# Optimizing a Trainium2 kernel written in Bass

```python
import math
import numpy as np
import jax
import jax.numpy as jnp
from jax import lax

D_MODEL = 1024
BATCH = 1
SEQ = 256
DEPTH = 2
DEC_BATCH = 1
DEC_SEQ = 64
PAST_LEN = 256

CHUNK = 64
Q_BLOCK = 128
EPS = 1e-6
NEG_INF = -1e30

H_A = 4
DK_A = 32
DV_A = 64
GLA_RANK = 16
GLA_TAU = 16.0
H_D = 4
DK_D = 64
DV_D = 128
H_R = 4
DK_R = 64
DV_R = 64
ROPE_BASE = 10000.0
D_FF = 2816

W_GLA = H_A * DV_A
W_DIFF = H_D * DV_D
W_RET = H_R * DV_R
D_MIX = W_GLA + W_DIFF + W_RET
IN_SPLITS = (GLA_RANK, H_A * DK_A, H_A * DK_A, W_GLA, W_GLA,
             2 * H_D * DK_D, 2 * H_D * DK_D, W_DIFF,
             H_R * DK_R, H_R * DK_R, W_RET, W_RET)
D_IN = 3344

kernel_name = 'hymba_gla_diff_retention_macaron_step'

def _rms_norm(x, g):
    xf = x.astype(jnp.float32)
    y = xf * lax.rsqrt(jnp.mean(xf * xf, axis=-1, keepdims=True) + EPS)
    return (y * g.astype(jnp.float32)).astype(x.dtype)

def _layer_norm(x, g):
    xf = x.astype(jnp.float32)
    xc = xf - jnp.mean(xf, axis=-1, keepdims=True)
    y = xc * lax.rsqrt(jnp.mean(xc * xc, axis=-1, keepdims=True) + EPS)
    return (y * g.astype(jnp.float32)).astype(x.dtype)

def _swiglu(h, w_up, w_down):
    gate, up = jnp.split(h @ w_up, 2, axis=-1)
    return (jax.nn.silu(gate) * up) @ w_down

def _to_chunks(x, c):
    b, t, h, d = x.shape
    return x.reshape(b, t // c, c, h, d).transpose(1, 0, 3, 2, 4)

def _from_chunks(o):
    n, b, h, c, d = o.shape
    return o.transpose(1, 0, 3, 2, 4).reshape(b, n * c, h, d)

def _rotary(x, pos):
    half = x.shape[-1] // 2
    inv = ROPE_BASE ** (-jnp.arange(half, dtype=jnp.float32) / half)
    ang = pos.astype(jnp.float32)[:, None] * inv[None, :]
    cos = jnp.cos(ang)[None, :, None, :]
    sin = jnp.sin(ang)[None, :, None, :]
    xf = x.astype(jnp.float32)
    x1, x2 = xf[..., :half], xf[..., half:]
    return jnp.concatenate([x1 * cos - x2 * sin, x1 * sin + x2 * cos], axis=-1).astype(x.dtype)

def _gla_chunked(q, k, v, log_a, s0):
    t = q.shape[1]
    c = min(CHUNK, t)
    tri = jnp.tril(jnp.ones((c, c), dtype=bool))

    def step(s, inp):
        qc, kc, vc, ac = inp
        b = jnp.cumsum(ac, axis=2)
        rel = jnp.where(tri[:, :, None], b[:, :, :, None, :] - b[:, :, None, :, :], -jnp.inf)
        scores = jnp.einsum('bhtsd,bhsd->bhts', qc[:, :, :, None, :] * jnp.exp(rel), kc)
        o = jnp.einsum('bhts,bhsv->bhtv', scores, vc) + jnp.einsum('bhtd,bhdv->bhtv', qc * jnp.exp(b), s)
        b_last = b[:, :, -1]
        s_new = jnp.exp(b_last)[..., None] * s + jnp.einsum(
            'bhsd,bhsv->bhdv', kc * jnp.exp(b_last[:, :, None, :] - b), vc)
        return s_new, o

    xs = tuple(_to_chunks(a.astype(jnp.float32), c) for a in (q, k, v, log_a))
    s_fin, o = lax.scan(step, s0.astype(jnp.float32), xs)
    return _from_chunks(o), s_fin.astype(s0.dtype)

def _retention_chunked(q, k, v, s0):
    t = q.shape[1]
    c = min(CHUNK, t)
    lg = jnp.log(1.0 - 2.0 ** (-5.0 - jnp.arange(H_R, dtype=jnp.float32)))
    idx = jnp.arange(c, dtype=jnp.float32)
    tri = idx[:, None] >= idx[None, :]
    dec = jnp.exp(jnp.where(tri[None], (idx[:, None] - idx[None, :])[None] * lg[:, None, None], -jnp.inf))
    q_dec = jnp.exp((idx[None, :] + 1.0) * lg[:, None])
    k_dec = jnp.exp((c - 1.0 - idx[None, :]) * lg[:, None])
    c_dec = jnp.exp(c * lg)

    def step(s, inp):
        qc, kc, vc = inp
        scores = jnp.einsum('bhtd,bhsd->bhts', qc, kc) * dec[None]
        o = jnp.einsum('bhts,bhsv->bhtv', scores, vc) + jnp.einsum(
            'bhtd,bhdv->bhtv', qc * q_dec[None, :, :, None], s)
        s_new = c_dec[None, :, None, None] * s + jnp.einsum(
            'bhsd,bhsv->bhdv', kc * k_dec[None, :, :, None], vc)
        return s_new, o

    xs = tuple(_to_chunks(a.astype(jnp.float32), c) for a in (q, k, v))
    s_fin, o = lax.scan(step, s0.astype(jnp.float32), xs)
    return _from_chunks(o), s_fin.astype(s0.dtype)

def _diff_attention(q, k, v, q_pos, k_pos, lam):
    b, tq = q.shape[0], q.shape[1]
    qb = min(Q_BLOCK, tq)
    nb = tq // qb
    kf = k.astype(jnp.float32) * DK_D ** -0.5
    vf = v.astype(jnp.float32)
    slopes = 2.0 ** (-8.0 * jnp.arange(1, H_D + 1, dtype=jnp.float32) / H_D)
    k_chunk = k_pos // CHUNK
    q_blocks = q.astype(jnp.float32).reshape(b, nb, qb, H_D, 2, DK_D).swapaxes(0, 1)
    p_blocks = q_pos.reshape(nb, qb)

    def one_block(args):
        qblk, pblk = args
        s = jnp.einsum('bqhmd,bkhmd->bmhqk', qblk, kf)
        dist = jnp.abs(pblk[:, None] - k_pos[None, :]).astype(jnp.float32)
        visible = k_chunk[None, :] <= (pblk // CHUNK)[:, None]
        s = jnp.where(visible, s - slopes[:, None, None] * dist, NEG_INF)
        p = jax.nn.softmax(s, axis=-1)
        a = p[:, 0] - lam * p[:, 1]
        return jnp.einsum('bhqk,bkhv->bqhv', a, vf)

    o = lax.map(one_block, (q_blocks, p_blocks))
    return o.swapaxes(0, 1).reshape(b, tq, H_D, DV_D)

def _mixer(h, l, P, past_k, past_v, s_gla0, s_ret0):
    b, t, _ = h.shape
    past_len = 0 if past_k is None else past_k.shape[1]
    pos = past_len + jnp.arange(t)
    z = h @ P['w_in'][l]
    offs = [int(o) for o in np.cumsum(IN_SPLITS)[:-1]]
    a_lr, gq, gk, gv, gr, dq, dk, dv, rq, rk, rv, rg = jnp.split(z, offs, axis=-1)

    q_a = gq.reshape(b, t, H_A, DK_A) * DK_A ** -0.5
    k_a = gk.reshape(b, t, H_A, DK_A)
    v_a = gv.reshape(b, t, H_A, DV_A)
    log_a = jax.nn.log_sigmoid((a_lr @ P['w_gla_a2'][l] + P['b_gla_a'][l]).astype(jnp.float32)) / GLA_TAU
    o_a, s_gla = _gla_chunked(q_a, k_a, v_a, log_a.reshape(b, t, H_A, DK_A), s_gla0)
    o_a = _rms_norm(o_a.astype(h.dtype), P['gla_norm'][l]).reshape(b, t, W_GLA) * jax.nn.silu(gr)

    q_d = dq.reshape(b, t, H_D, 2, DK_D)
    k_rows = dk.reshape(b, t, H_D, 2 * DK_D)
    v_rows = dv.reshape(b, t, H_D, DV_D)
    if past_k is None:
        k_all, v_all = k_rows, v_rows
    else:
        k_all = jnp.concatenate([past_k.astype(k_rows.dtype), k_rows], axis=1)
        v_all = jnp.concatenate([past_v.astype(v_rows.dtype), v_rows], axis=1)
    lam_p = P['diff_lambda'][l].astype(jnp.float32)
    lam_init = 0.8 - 0.6 * math.exp(-0.3 * l)
    lam = jnp.exp(jnp.sum(lam_p[0] * lam_p[1])) - jnp.exp(jnp.sum(lam_p[2] * lam_p[3])) + lam_init
    o_d = _diff_attention(q_d, k_all.reshape(b, past_len + t, H_D, 2, DK_D), v_all,
                          pos, jnp.arange(past_len + t), lam)
    o_d = (_rms_norm(o_d.astype(h.dtype), P['diff_subln'][l]) * (1.0 - lam_init)).reshape(b, t, W_DIFF)

    q_r = _rotary(rq.reshape(b, t, H_R, DK_R), pos)
    k_r = _rotary(rk.reshape(b, t, H_R, DK_R), pos) * DK_R ** -0.5
    v_r = rv.reshape(b, t, H_R, DV_R)
    o_r, s_ret = _retention_chunked(q_r, k_r, v_r, s_ret0)
    o_r = _layer_norm(o_r.astype(h.dtype), P['ret_norm'][l]).reshape(b, t, W_RET) * jax.nn.silu(rg)

    out = jnp.concatenate([o_a, o_d, o_r], axis=-1) @ P['w_out'][l]
    return out, k_rows, v_rows, s_gla, s_ret

def _layer(x, l, P, past_k, past_v, s_gla0, s_ret0):
    h = _rms_norm(x, P['ffn1_norm_pre'][l])
    x = x + 0.5 * _rms_norm(_swiglu(h, P['ffn1_w_up'][l], P['ffn1_w_down'][l]), P['ffn1_norm_post'][l])
    h = _rms_norm(x, P['mix_norm_pre'][l])
    m, k_rows, v_rows, s_gla, s_ret = _mixer(h, l, P, past_k, past_v, s_gla0, s_ret0)
    x = x + _rms_norm(m, P['mix_norm_post'][l])
    h = _rms_norm(x, P['ffn2_norm_pre'][l])
    x = x + 0.5 * _rms_norm(_swiglu(h, P['ffn2_w_up'][l], P['ffn2_w_down'][l]), P['ffn2_norm_post'][l])
    return x, k_rows, v_rows, s_gla, s_ret

def setup_inputs(seed: int = 0) -> dict:
    key = jax.random.key(seed)
    ks = jax.random.split(key, 24)
    f32 = jnp.float32

    def nrm(k, shape, scale):
        return jax.random.normal(k, shape, f32) * scale

    def gain(k, shape):
        return 1.0 + 0.05 * jax.random.normal(k, shape, f32)

    return {
        'x_prompt': nrm(ks[0], (BATCH, SEQ, D_MODEL), 1.0),
        'x_sample': nrm(ks[1], (DEC_BATCH, DEC_SEQ, D_MODEL), 1.0),
        'cache_diff_k': nrm(ks[2], (DEPTH, DEC_BATCH, PAST_LEN, H_D, 2 * DK_D), 1.0),
        'cache_diff_v': nrm(ks[3], (DEPTH, DEC_BATCH, PAST_LEN, H_D, DV_D), 1.0),
        'state_gla': nrm(ks[4], (DEPTH, DEC_BATCH, H_A, DK_A, DV_A), 1.0),
        'state_ret': nrm(ks[5], (DEPTH, DEC_BATCH, H_R, DK_R, DV_R), 1.0),
        'ffn1_norm_pre': gain(ks[6], (DEPTH, D_MODEL)),
        'ffn1_w_up': nrm(ks[7], (DEPTH, D_MODEL, 2 * D_FF), D_MODEL ** -0.5),
        'ffn1_w_down': nrm(ks[8], (DEPTH, D_FF, D_MODEL), D_FF ** -0.5),
        'ffn1_norm_post': gain(ks[9], (DEPTH, D_MODEL)),
        'mix_norm_pre': gain(ks[10], (DEPTH, D_MODEL)),
        'w_in': nrm(ks[11], (DEPTH, D_MODEL, D_IN), D_MODEL ** -0.5),
        'w_gla_a2': nrm(ks[12], (DEPTH, GLA_RANK, H_A * DK_A), GLA_RANK ** -0.5),
        'b_gla_a': nrm(ks[13], (DEPTH, H_A * DK_A), 0.1),
        'gla_norm': gain(ks[14], (DEPTH, H_A, DV_A)),
        'diff_lambda': nrm(ks[15], (DEPTH, 4, DK_D), 0.1),
        'diff_subln': gain(ks[16], (DEPTH, DV_D)),
        'ret_norm': gain(ks[17], (DEPTH, H_R, DV_R)),
        'w_out': nrm(ks[18], (DEPTH, D_MIX, D_MODEL), D_MIX ** -0.5),
        'mix_norm_post': gain(ks[19], (DEPTH, D_MODEL)),
        'ffn2_norm_pre': gain(ks[20], (DEPTH, D_MODEL)),
        'ffn2_w_up': nrm(ks[21], (DEPTH, D_MODEL, 2 * D_FF), D_MODEL ** -0.5),
        'ffn2_w_down': nrm(ks[22], (DEPTH, D_FF, D_MODEL), D_FF ** -0.5),
        'ffn2_norm_post': gain(ks[23], (DEPTH, D_MODEL)),
    }

def reference(x_prompt, x_sample, cache_diff_k, cache_diff_v, state_gla, state_ret,
              ffn1_norm_pre, ffn1_w_up, ffn1_w_down, ffn1_norm_post,
              mix_norm_pre, w_in, w_gla_a2, b_gla_a, gla_norm, diff_lambda, diff_subln,
              ret_norm, w_out, mix_norm_post,
              ffn2_norm_pre, ffn2_w_up, ffn2_w_down, ffn2_norm_post):
    P = {
        'ffn1_norm_pre': ffn1_norm_pre, 'ffn1_w_up': ffn1_w_up, 'ffn1_w_down': ffn1_w_down,
        'ffn1_norm_post': ffn1_norm_post, 'mix_norm_pre': mix_norm_pre, 'w_in': w_in,
        'w_gla_a2': w_gla_a2, 'b_gla_a': b_gla_a, 'gla_norm': gla_norm, 'diff_lambda': diff_lambda,
        'diff_subln': diff_subln, 'ret_norm': ret_norm, 'w_out': w_out, 'mix_norm_post': mix_norm_post,
        'ffn2_norm_pre': ffn2_norm_pre, 'ffn2_w_up': ffn2_w_up, 'ffn2_w_down': ffn2_w_down,
        'ffn2_norm_post': ffn2_norm_post,
    }
    bp = x_prompt.shape[0]
    xp, xs = x_prompt, x_sample
    kp, vp, gp, rp = [], [], [], []
    ksm, vsm, gsm, rsm = [], [], [], []
    for l in range(DEPTH):
        xp, k_, v_, g_, r_ = _layer(xp, l, P, None, None,
                                    jnp.zeros((bp, H_A, DK_A, DV_A), x_prompt.dtype),
                                    jnp.zeros((bp, H_R, DK_R, DV_R), x_prompt.dtype))
        kp.append(k_); vp.append(v_); gp.append(g_); rp.append(r_)
        xs, k_, v_, g_, r_ = _layer(xs, l, P, cache_diff_k[l], cache_diff_v[l], state_gla[l], state_ret[l])
        ksm.append(k_); vsm.append(v_); gsm.append(g_); rsm.append(r_)
    new_k_prompt = jnp.stack(kp)
    new_v_prompt = jnp.stack(vp)
    state_gla_prompt = jnp.stack(gp)
    state_ret_prompt = jnp.stack(rp)
    new_k_sample = jnp.stack(ksm)
    new_v_sample = jnp.stack(vsm)
    state_gla_sample = jnp.stack(gsm)
    state_ret_sample = jnp.stack(rsm)
    return (xp, xs, new_k_prompt, new_v_prompt, state_gla_prompt, state_ret_prompt,
            new_k_sample, new_v_sample, state_gla_sample, state_ret_sample)


_drawn_inputs = setup_inputs


def setup_inputs(seed=0):
    import zlib

    import numpy as np

    out = dict(_drawn_inputs(seed))
    spreads = {}
    factors = {'diff_lambda': 3.473}
    for name, (base, spread) in spreads.items():
        noise = np.random.default_rng([zlib.crc32(name.encode()), seed]).standard_normal(out[name].shape)
        drawn = base * np.exp(spread * noise) if base else spread * noise
        out[name] = jnp.asarray(drawn.astype(out[name].dtype))
    for name, factor in factors.items():
        out[name] = (out[name] * factor).astype(out[name].dtype)
    return out
```

```python
from contextlib import ExitStack

import numpy as np
import concourse.bass as bass
from concourse import mybir

F32 = mybir.dt.float32
F32R = mybir.dt.float32r
U8 = mybir.dt.uint8
ACT = mybir.ActivationFunctionType
ALU = mybir.AluOpType
AX = mybir.AxisListType

P = 128
DEPTH, D, D_FF, D_IN = 2, 1024, 2816, 3344
T_P, T_S, PAST = 256, 64, 256
T = T_P + T_S
KD = D // P
KF = D_FF // P
TOK = (0, 128, 192)
EPS = 1e-6
RANK, H, DK_A, DV_A, DK_D, DV_D, DK_R, DV_R = 16, 4, 32, 64, 64, 128, 64, 64
HALF_DOWN = KF // 2

N_UP, N_DOWN, N_MIX, N_OUT = KF, 2 * KD, 14, KD // 2
U_F1, U_MIX = 0, N_UP + N_DOWN
U_OUT = U_MIX + N_MIX
U_F2 = U_OUT + N_OUT
UNITS = U_F2 + N_UP + N_DOWN
G_F1, G_MIX = 0, N_UP + KD
G_OUT = G_MIX + N_MIX
G_F2 = G_OUT + N_OUT
GROUPS = G_F2 + N_UP + KD

GQ, GK, GV, GR, DQ, DKK, DV, RQ, RK, RV, RG = 0, 1, 2, 4, 6, 10, 14, 18, 20, 22, 24
NZ = 26
LEVELS = (128, 64, 32, 16, 8, 4, 2, 1, 0)
SPLITS = ((DKK, 0), (DKK + 1, 1), (DKK + 2, 2), (DKK + 3, 3), (DV, 0), (DV + 1, 1), (DV + 2, 2), (DV + 3, 3),
          (GV, 0), (GV + 1, 1), (RV, 0), (RV + 1, 1))
ATT = [(h, b) for h in range(H) for b in range(3)]
KEYS = (1, 2, 3)
BIAS_AT = (0, 128, 384)


def milestones():
    pe, act, dve = [], [], []
    pe += ["kct0", "kct1"]
    act += ["kct0", "kct1"]
    for n in range(12):
        pe.append(f"tok{n}")
        act.append(f"tok{n}")
    pe.append("logit")
    act += ["abs", "softplus"]
    dve += ["minus", "decay"]
    for n in range(8):
        dve += [f"dist{n}", f"qk{n}", f"score{n}"]
        act.append(f"weight{n}")
        pe.append(f"level{n}")
    dve.append("score8")
    pe.append("level8")
    act += ["from_start", "to_end"]
    dve += ["q_start", "k_end"]
    pe += ["ketok", "gla_state", "gla_o"]
    act += ["ketok"]
    dve += ["gla_state", "gla_o"]
    act += ["gla_sq", "gla_sqrt", "gla_gate"]
    pe += ["gla_ms"]
    dve += ["gla_var", "gla_done"]
    for i in range(12):
        pe += [f"att_s{i}", f"att_t{i}", f"att_o{i}"]
        dve += [f"att_max{i}", f"att_a{i}"]
        act += [f"att_e{i}", f"att_t{i}"]
        if i % 3 == 2:
            act.append(f"att_o{i}")
    for h in range(H):
        act += [f"att_sq{h}", f"att_sqrt{h}"]
        pe.append(f"att_ms{h}")
        dve += [f"att_var{h}", f"att_done{h}"]
    for j in range(4):
        pe.append(f"rot{j}")
        dve.append(f"rot{j}")
    for h in range(H):
        pe.append(f"ret_s{h}")
        dve.append(f"ret_s{h}")
    dve += ["ret_q", "ret_k"]
    pe += ["ret_kt0", "ret_kt1", "ret_state", "ret_o", "ret_mu", "ret_ms"]
    act += ["ret_kt0", "ret_kt1", "ret_sq", "ret_sqrt", "ret_gate"]
    dve += ["ret_state", "ret_o", "ret_xc", "ret_var", "ret_done"]
    return {"pe": pe, "act": act, "dve": dve}


MILESTONES = milestones()


def constants():
    parts, at = [], {}

    def add(name, a):
        at[name] = (sum(x.shape[1] for x in parts), a.shape[1])
        parts.append(a.astype(np.float32))

    r = np.arange(P)
    add("ident", np.eye(P))
    add("ones", np.ones((P, P)))
    add("mean64", np.kron(np.eye(2), np.ones((64, 64))) / 64.0)
    add("mean128", np.ones((P, P)) / 128.0)
    rot = np.zeros((P, P))
    for g in (0, 64):
        for i in range(32):
            rot[g + 32 + i, g + i] = -1.0
            rot[g + i, g + 32 + i] = 1.0
    add("rot", rot)
    pos = np.concatenate([np.arange(T_P), PAST + np.arange(T_S)]).astype(np.float32)
    inv = np.float32(10000.0) ** (-np.arange(32, dtype=np.float32) / np.float32(32))
    ang = pos[None, :] * inv[r % 32][:, None]
    add("cos", np.cos(ang.astype(np.float32)))
    add("sin", np.sin(ang.astype(np.float32)))
    lg = np.log(1.0 - 2.0 ** (-5.0 - np.arange(H)))
    loc = np.concatenate([np.arange(T_P), np.arange(T_S)])
    last = np.concatenate([np.full(T_P, T_P - 1), np.full(T_S, T_S - 1)])
    for j in range(2):
        add(f"k_dec{j}", np.exp((last - loc)[None, :] * lg[2 * j + r // 64][:, None]))
    for j in range(2):
        add(f"q_dec{j}", np.exp((np.arange(T_S) + 1.0)[None, :] * lg[2 * j + r // 64][:, None]))
    for h in range(H):
        dt = r[None, :] - r[:, None]
        diag = np.where(dt >= 0, np.exp(np.maximum(dt, 0) * lg[h]), 0.0)
        samp = np.where((r[:, None] >= 64) & (r[None, :] >= 64), diag, 0.0)
        add(f"dec{h}", np.concatenate([diag, samp, diag, np.exp((dt + 128) * lg[h])], axis=1))
    for h in range(H):
        slope = 2.0 ** (-8.0 * (h + 1) / H)

        def bias(qp, kp):
            b = -slope * np.abs(qp[:, None] - kp[None, :])
            return np.where(kp[None, :] // 64 <= qp[:, None] // 64, b, -1e30)

        b2 = bias(PAST + r % 64, np.concatenate([np.arange(PAST), PAST - 64 + r]))
        b2[:, PAST:PAST + 64] = -1e30
        add(f"bias{h}", np.concatenate([bias(r, r), bias(128 + r, np.arange(256)), b2], axis=1))
    lam = 0.8 - 0.6 * np.exp(-0.3 * np.arange(DEPTH))
    add("lam", np.tile(np.concatenate([lam, 1.0 - lam])[None, :], (P, 1)))
    add("eps", np.full((P, 1), EPS))
    add("ones_row", np.ones((P, T_P)))
    masks = []
    for c in LEVELS[1:]:
        if c:
            m = (r[:, None] // (2 * c) == r[None, :] // (2 * c)) & (r[:, None] % (2 * c) < c) & (r[None, :] % (2 * c) >= c)
        else:
            m = r[:, None] == r[None, :]
        s = m & (r[:, None] >= 64) & (r[None, :] >= 64)
        masks.append(np.concatenate([m, s, m], axis=1))
    return np.concatenate(parts, axis=1), at, np.concatenate(masks, axis=1).astype(np.float32)


def build(nc, ins, outs, table_at):
    ctx = ExitStack()
    with ctx:
        total = [0]

        def sb(name, shape, dt=F32):
            return ctx.enter_context(nc.sbuf_tensor(name, shape, dt))

        def sem(name):
            return ctx.enter_context(nc.semaphore(name))

        raw = [sb(f"raw{s}", [P, 16 * P]) for s in range(2)]
        w_h = [sb(f"w_h{s}", [P, 16 * P], F32R) for s in range(2)]
        w_l = [sb(f"w_l{s}", [P, 16 * P], F32R) for s in range(2)]
        x = sb("x", [P, KD, T])
        y = sb("y", [P, KD, T])
        NCONST = sum(n for _, n in table_at.values())
        const = sb("const", [P, NCONST])
        mask = sb("mask", [P, 8, 3 * P], U8)
        gains = sb("gains", [P, DEPTH, 6, KD])
        small = sb("small", [P, DEPTH, 8])
        a2 = sb("a2", [RANK, DEPTH, P])
        lam_in = sb("lam_in", [P, DEPTH, 4, DK_D])
        lam_p = sb("lam_p", [P, DEPTH * 2, DK_D])
        lam_e = sb("lam_e", [P, DEPTH * 2])
        lam_all = sb("lam_all", [P, DEPTH])
        gain_l = sb("gain_l", [P, 6, KD])
        small_l = sb("small_l", [P, 8])
        a2_l = sb("a2_l", [RANK, P])
        rs = sb("rs", [P, T])
        var = sb("var", [P, T])
        ssum = sb("ssum", [P, T])
        sq = [sb(f"sq{s}", [P, T]) for s in range(2)]

        base = nc.sbuf_base
        room = nc.sbuf_usable_end - base

        def placer(start):
            here = [start]

            def place(name, shape, dt=F32):
                size = (1 if dt == U8 else 4) * int(np.prod(shape[1:]))
                t = nc.alloc_sbuf_tensor_at(name, shape, dt, offset=here[0])
                here[0] += (size + 31) // 32 * 32
                return t
            return place, here

        place, here = placer(base)
        xn_h = place("xn_h", [P, KD, T], F32R)
        xn_l = place("xn_l", [P, KD, T], F32R)
        region = here[0]
        place, here2 = placer(base)
        dk_tok = place("dk_tok", [P, 3, H, P])
        rv_tok = place("rv_tok", [P, 3, 256])
        rk_tok = place("rk_tok", [P, 3, 256])
        assert here2[0] <= region
        place, here = placer(region)
        hid_h = place("hid_h", [P, KF, T], F32R)
        hid_l = place("hid_l", [P, KF, T], F32R)
        gate = [place(f"gate{s}", [P, T]) for s in range(2)]
        up = [place(f"up{s}", [P, T]) for s in range(2)]
        assert here[0] <= nc.sbuf_usable_end
        place, here = placer(region)
        x_in = place("x_in", [P, 3, D])
        mask_in = place("mask_in", [P, 8 * 3 * P])
        place, here = placer(region)
        z = place("z", [P, NZ, T])
        alr = place("alr", [P, T])
        dv_tok = place("dv_tok", [P, 3, H, P])
        gv_tok = place("gv_tok", [P, 3, 256])
        scores = place("scores", [P, H, 4, P])
        probs = place("probs", [P, 2, 2, 3 * P])
        probs_t = place("probs_t", [P, 3, P])
        kc_t = place("kc_t", [P, H, PAST])
        vc = place("vc", [P, 2, H * P])
        decay = place("decay", [P, T])
        wgt = place("wgt", [P, T])
        q_w = place("q_w", [P, T])
        k_w = place("k_w", [P, T])
        s0_a = place("s0_a", [P, DV_A])
        s0_r = place("s0_r", [P, 2, DV_R])
        q_s = place("q_s", [P, 2, T_S])
        st_a = place("st_a", [P, 2, DV_A])
        st_r = place("st_r", [P, 2, 2, DV_R])
        tiny = place("tiny", [P, 32])
        gk_tok = place("gk_tok", [P, 3, P])
        assert here[0] <= nc.sbuf_usable_end, (here[0], nc.sbuf_usable_end)
        kc_raw = scores[:, :, :, :].rearrange("p h b c -> p (h b c)")[:, 0:2 * H * P].rearrange("p (i c) -> p i c", i=2)

        ps_g = ctx.enter_context(nc.psum_tensor("ps_g", [P, 4, 512], F32))
        ps_m = ctx.enter_context(nc.psum_tensor("ps_m", [P, 4, 512], F32))

        def C(name):
            a, n = table_at[name]
            return const[:, a:a + n]

        loaded = sem("tables_loaded")
        x_loaded = sem("x_loaded")
        raw_in = [sem(f"raw_in{s}") for s in range(2)]
        w_hi, w_lo, w_used = sem("w_hi"), sem("w_lo"), sem("w_used")
        evac = sem("evac")
        x_new = sem("x_new")
        xn_hi, xn_lo = sem("xn_hi"), sem("xn_lo")
        sq_x = sem("sq_x")
        ss_in = sem("ss_in")
        ss_mm = sem("ss_mm")
        ss_var = sem("ss_var")
        ss_sqrt = sem("ss_sqrt")
        rs_out = sem("rs_out")
        up_mul, silu, prod = sem("gate_scaled"), sem("silu_done"), sem("hidden_product")
        hid_hi, hid_lo = sem("hid_hi"), sem("hid_lo")
        y_sq = sem("y_sq")
        y_acc = sem("y_acc")
        past_in = sem("past_in")
        kv_stored, st_stored = sem("keys_and_values_stored"), sem("states_stored")
        params = sem("params")
        y_stored = sem("y_stored")
        passed = sem("passed")
        y_mm, y_rows = sem("y_mm"), sem("y_rows")
        x_mm = sem("x_mm")
        mem_set = sem("scores_zeroed")
        lam_s = sem("lam_s")
        mix = {k: sem(f"mix_{k}") for k in ("pe", "act", "dve")}
        place_of = {k: {name: n + 1 for n, name in enumerate(v)} for k, v in MILESTONES.items()}
        reached = {"pe": 0, "act": 0, "dve": 0}

        def mark(who, instruction, name):
            reached[who] += 1
            assert place_of[who][name] == reached[who], (who, name, MILESTONES[who][reached[who] - 1])
            instruction.then_inc(mix[who], 1)

        def after(e, l, who, name):
            e.wait_ge(mix[who], l * len(MILESTONES[who]) + place_of[who][name])

        def then_pass(e):
            e.sem_inc(passed, 1)

        block = ctx.enter_context(nc.Block())
        rearr = lambda t: t[:, :, :].rearrange("p a b -> p (a b)")

        @block.sync
        def _(sp):
            def load(l, u, s, src, k, c):
                sp.wait_ge(w_lo, l * UNITS + u + 1)
                dst = raw[s][:, 0:k * c].rearrange("p (k c) -> p k c", k=k)
                sp.dma_start(dst, src).then_inc(raw_in[s], 16)

            def rows(w, l, r0, nk, c0, nc_):
                return w[bass.ds(l, 1), r0:r0 + nk * P, c0].rearrange("a (k p) c -> p (a k) c", p=P)

            def ffn(l, u0, w_up, w_down):
                with sp.Fori(0, N_UP // 2) as j:
                    for s in range(2):
                        sp.wait_ge(w_lo, l * UNITS + (2 * j + (u0 + s + 1)))
                        dst = raw[s][:, :].rearrange("p (g k c) -> p g k c", g=2, k=KD)
                        for g in range(2):
                            src = w_up[bass.ds(l, 1), :, bass.ds(2 * P * j + (g * D_FF + s * P), P)]
                            ins_ = sp.dma_start(dst[:, g], src.rearrange("a (k p) c -> p (a k) c", p=P))
                            ins_.then_inc(raw_in[s], 16)
                with sp.Fori(0, KD) as m:
                    for s in range(2):
                        src = w_down[bass.ds(l, 1), s * HALF_DOWN * P:(s + 1) * HALF_DOWN * P, bass.ds(P * m, P)]
                        load(l, 2 * m + (u0 + N_UP + s), s, src.rearrange("a (k p) c -> p (a k) c", p=P), HALF_DOWN, P)

            def pairs(l, u0, n, w, c0):
                with sp.Fori(0, n // 2) as j:
                    for s in range(2):
                        src = w[bass.ds(l, 1), :, bass.ds(4 * P * j + (c0 + 2 * s * P), 2 * P)]
                        load(l, 2 * j + (u0 + s), s, src.rearrange("a (k p) c -> p (a k) c", p=P), KD, 2 * P)

            with sp.Fori(0, DEPTH) as l:
                ffn(l, U_F1, ins["ffn1_w_up"], ins["ffn1_w_down"])
                w = ins["w_in"]
                load(l, U_MIX, 0, w[bass.ds(l, 1), :, 0:P].rearrange("a (k p) c -> p (a k) c", p=P), KD, P)
                load(l, U_MIX + 1, 1, w[bass.ds(l, 1), :, RANK:RANK + 2 * P].rearrange("a (k p) c -> p (a k) c", p=P), KD, 2 * P)
                pairs(l, U_MIX + 2, N_MIX - 2, w, RANK + 2 * P)
                pairs(l, U_OUT, N_OUT, ins["w_out"], 0)
                ffn(l, U_F2, ins["ffn2_w_up"], ins["ffn2_w_down"])

        RAW = [0] * (UNITS + 1)
        def raw_after(u):
            tot = 0
            for v in range(u % 2, u + 1, 2):
                up_unit = v < N_UP or U_F2 <= v < U_F2 + N_UP
                tot += 32 if up_unit else 16
            return tot
        RAW_LAYER = raw_after(UNITS - 1)
        assert raw_after(UNITS - 2) == RAW_LAYER

        @block.gpsimd
        def _(pool):
            pool.dma_start(const[:, :], ins["tables"]).then_inc(loaded, 16)
            pool.dma_start(mask_in[:, :], ins["masks"]).then_inc(loaded, 16)
            for n, name in enumerate(("ffn1_norm_pre", "ffn1_norm_post", "mix_norm_pre", "mix_norm_post",
                                      "ffn2_norm_pre", "ffn2_norm_post")):
                for l in range(DEPTH):
                    pool.dma_start(gains[:, l, n, :], ins[name][l].rearrange("(k p) -> p k", p=P),
                                   allow_slow_non_contiguous=True).then_inc(loaded, 16)
            for l in range(DEPTH):
                col = lambda a: a.rearrange("(p o) -> p o", o=1)
                pool.dma_start(small[:, l, 0:1], col(ins["b_gla_a"][l])).then_inc(loaded, 16)
                pool.dma_start(small[:, l, 1:3], ins["gla_norm"][l].rearrange("(j h) v -> (h v) j", j=2),
                               allow_slow_non_contiguous=True).then_inc(loaded, 16)
                pool.dma_start(small[:, l, 3:4], col(ins["diff_subln"][l])).then_inc(loaded, 16)
                pool.dma_start(small[:, l, 4:6], ins["ret_norm"][l].rearrange("(j h) v -> (h v) j", j=2),
                               allow_slow_non_contiguous=True).then_inc(loaded, 16)
                pool.dma_start(a2[:, l, :], ins["w_gla_a2"][l]).then_inc(loaded, 16)
                pool.dma_start(lam_in[:, l, :, :].rearrange("p a b -> p (a b)"),
                               ins["diff_lambda"][l:l + 1].rearrange("o a b -> o (a b)").broadcast_to([P, 4 * DK_D])
                               ).then_inc(loaded, 16)
            with pool.Fori(0, DEPTH) as l:
                pool.wait_ge(w_used, l * UNITS + (U_MIX + 2))
                then_pass(pool)
                pool.dma_start(kc_raw, ins["cache_diff_k"][bass.ds(l, 1), 0].rearrange("a (i p) h d -> p (a i) (h d)", p=P)
                               ).then_inc(past_in, 16)
                pool.dma_start(vc[:, :, :], ins["cache_diff_v"][bass.ds(l, 1), 0].rearrange("a (i p) h d -> p (a i) (h d)", p=P)
                               ).then_inc(past_in, 16)
                pool.dma_start(s0_a[:, :], ins["state_gla"][bass.ds(l, 1), 0].rearrange("a h d v -> (a h d) v")
                               ).then_inc(past_in, 16)
                pool.dma_start(s0_r[:, :, :], ins["state_ret"][bass.ds(l, 1), 0].rearrange("a (j h) d v -> (a h d) j v", j=2)
                               ).then_inc(past_in, 16)
                after(pool, l, "pe", "kct1")
                then_pass(pool)
                pool.memset(scores[:, :, :, :], 0.0).then_inc(mem_set, 1)
                after(pool, l, "act", "tok7")
                then_pass(pool)
                for t, name in ((dk_tok, "k"), (dv_tok, "v")):
                    o = outs[f"new_{name}_prompt"]
                    pool.dma_start(o[bass.ds(l, 1), 0].rearrange("a (i p) h d -> p (a i) (h d)", p=P),
                                   t[:, 0:2, :, :].rearrange("p i h d -> p i (h d)")).then_inc(kv_stored, 16)
                    o = outs[f"new_{name}_sample"]
                    pool.dma_start(o[bass.ds(l, 1), 0].rearrange("a p h d -> p (a h d)"),
                                   t[64:128, 2, :, :].rearrange("p h d -> p (h d)")).then_inc(kv_stored, 16)
                after(pool, l, "dve", "gla_state")
                then_pass(pool)
                for n, name in enumerate(("prompt", "sample")):
                    pool.dma_start(outs[f"state_gla_{name}"][bass.ds(l, 1), 0].rearrange("a h d v -> (a h d) v"),
                                   st_a[:, n, :]).then_inc(st_stored, 16)
                after(pool, l, "dve", "ret_state")
                then_pass(pool)
                for n, name in enumerate(("prompt", "sample")):
                    pool.dma_start(outs[f"state_ret_{name}"][bass.ds(l, 1), 0].rearrange("a (j h) d v -> (a h d) j v", j=2),
                                   st_r[:, n, :, :]).then_inc(st_stored, 16)
            pool.wait_ge(kv_stored, DEPTH * 4 * 16)
            pool.wait_ge(st_stored, DEPTH * 4 * 16)
        N_LOADED = 16 * (2 + 6 * DEPTH + 6 * DEPTH)

        @block.tensor
        def _(pe):
            pe.sem_inc(w_used, 2)

            def product(out, s, blk, xh, xl, first, last):
                w = slice(blk * P, blk * P + P)
                pe.matmul(out, w_h[s][:, w], xl, start=first, stop=False)
                pe.matmul(out, w_l[s][:, w], xh, start=False, stop=False)
                return pe.matmul(out, w_h[s][:, w], xh, start=False, stop=last)

            def unit_of_two(l, u, g, s, ready=None, tiles=2, k_major=False):
                pe.wait_ge(w_lo, l * UNITS + u + 3)
                pe.wait_ge(evac, l * GROUPS + g + 1)
                for k in range(KD):
                    if ready is not None:
                        ready(k)
                    for n in range(tiles):
                        blk = k * tiles + n if k_major else n * KD + k
                        mm = product(ps_g[:, 2 * s + n, 0:T], s, blk, xn_h[:, k, :], xn_l[:, k, :], k == 0, k == KD - 1)
                mm.then_inc(w_used, 1)

            def xn_ready(l, n):
                return lambda k: pe.wait_ge(xn_lo, l * 32 + (8 * n + k + 1))

            def sum_squares(l, n):
                pe.wait_ge(ss_in, l * 6 + n + 1)
                pe.matmul(ps_m[:, 0, 0:T], C("ones"), ssum[:, :], start=True, stop=True).then_inc(ss_mm, 1)

            def ffn(l, u0, g0, norm, xn):
                unit_of_two(l, u0, g0, 0, xn_ready(l, xn))
                sum_squares(l, norm)
                unit_of_two(l, u0 + 1, g0 + 1, 1)
                with pe.Fori(1, N_UP // 2) as j:
                    for s in range(2):
                        unit_of_two(l, 2 * j + (u0 + s), 2 * j + (g0 + s), s)
                with pe.Fori(0, KD // 2) as m:
                    for b in range(2):
                        for s in range(2):
                            pe.wait_ge(w_lo, l * UNITS + (4 * m + (u0 + N_UP + 2 * b + s + 3)))
                            if s == 0:
                                pe.wait_ge(evac, l * GROUPS + (2 * m + (g0 + N_UP + b + 1)))
                                pe.wait_ge(hid_lo, l * 2 * KF + (KF * (norm // 4) + HALF_DOWN))
                            else:
                                pe.wait_ge(hid_lo, l * 2 * KF + (KF * (norm // 4) + KF))
                            for i in range(HALF_DOWN):
                                k = s * HALF_DOWN + i
                                mm = product(ps_g[:, 2 * b, 0:T], s, i, hid_h[:, k, :], hid_l[:, k, :], k == 0, k == KF - 1)
                            mm.then_inc(w_used, 1)
                sum_squares(l, norm + 1)

            pe.wait_ge(loaded, N_LOADED)
            pe.wait_ge(x_loaded, 48)
            for k in range(KD):
                if k >= 2:
                    pe.wait_ge(x_new, k - 1)
                for i in range(3):
                    mm = pe.transpose(ps_m[:, k % 2, TOK[i]:TOK[i] + P], x_in[:, i, k * P:(k + 1) * P], C("ident"))
                mm.then_inc(x_mm, 1)

            with pe.Fori(0, DEPTH) as l:
                ffn(l, U_F1, G_F1, 0, 0)
                unit_of_two(l, U_MIX, G_MIX, 0, xn_ready(l, 1), tiles=1)
                sum_squares(l, 2)
                unit_of_two(l, U_MIX + 1, G_MIX + 1, 1, k_major=True)
                with pe.Fori(1, N_MIX // 2) as j:
                    for s in range(2):
                        unit_of_two(l, 2 * j + (U_MIX + s), 2 * j + (G_MIX + s), s, k_major=True)
                pe.wait_ge(evac, l * GROUPS + (G_MIX + N_MIX + 2))
                pe.wait_ge(past_in, (l + 1) * 64)
                for i in range(2):
                    for h in range(H):
                        mm = pe.transpose(ps_m[:, i, h * P:(h + 1) * P], kc_raw[:, i, h * P:(h + 1) * P], C("ident"))
                    mark("pe", mm, f"kct{i}")
                for n, (tile, _) in enumerate(SPLITS):
                    if n >= 2:
                        after(pe, l, "act", f"tok{n - 2}")
                    for i in range(3):
                        mm = pe.transpose(ps_m[:, 2 + n % 2, i * P:(i + 1) * P], z[:, tile, TOK[i]:TOK[i] + P], C("ident"))
                    mark("pe", mm, f"tok{n}")
                after(pe, l, "act", "kct1")
                mark("pe", pe.matmul(ps_m[:, 0, 0:T], a2_l[:, :], alr[0:RANK, :], start=True, stop=True), "logit")
                after(pe, l, "act", "tok11")
                for n, c in enumerate(LEVELS):
                    if n < 8:
                        after(pe, l, "dve", f"qk{n}")
                    if n:
                        after(pe, l, "dve", f"score{n - 1}")
                    for h in range(H):
                        r = slice(h * 32, h * 32 + 32)
                        todo = [(3, 0, 1)] if n == 0 else [(0, 1, 1), (2, 0, 0)] if n == 1 else [(0, 1, 1), (1, 2, 2), (2, 0, 0)]
                        for at, si, ti in todo:
                            qs, ks = (z[:, GQ, :], z[:, GK, :]) if c == 0 else (q_w[:, :], k_w[:, :])
                            mm = pe.matmul(ps_m[:, h, at * P:(at + 1) * P], ks[r, TOK[si]:TOK[si] + P],
                                           qs[r, TOK[ti]:TOK[ti] + P], start=True, stop=True)
                    mark("pe", mm, f"level{n}")
                after(pe, l, "dve", "k_end")
                after(pe, l, "dve", "score8")
                for i in range(3):
                    mm = pe.transpose(ps_m[:, 2, i * P:(i + 1) * P], k_w[:, TOK[i]:TOK[i] + P], C("ident"))
                mark("pe", mm, "ketok")
                after(pe, l, "act", "ketok")
                for n in range(2):
                    pe.matmul(ps_m[:, 0, 0:256], gk_tok[:, n, :], gv_tok[:, n, :], start=n == 0, stop=n == 1)
                mark("pe", pe.matmul(ps_m[:, 1, 0:256], gk_tok[64:128, 2, :], gv_tok[64:128, 2, :], start=True, stop=True),
                     "gla_state")

                def heads_out(bank0, v_tok, s0, q0, krows):
                    for h in range(H):
                        out = ps_m[64 * (h % 2):64 * (h % 2) + 64, bank0 + h // 2, :]
                        v = lambda i: v_tok[:, i, h * 64:(h + 1) * 64]
                        sc = scores[:, h, :, :].rearrange("p b c -> p (b c)")
                        kr, q = s0(h), q0(h)
                        pe.matmul(out[:, 0:256], v(0), sc[:, 256:512], start=True, stop=False, skip_group_check=True)
                        pe.matmul(out[:, 128:256], v(1), sc[:, 0:128], start=False, stop=False, skip_group_check=True)
                        pe.matmul(out[:, 256:320], v(2), sc[:, 192:256], start=False, stop=False, skip_group_check=True)
                        mm = pe.matmul(out[:, 256:320], kr, q, start=False, stop=True, skip_group_check=True)
                    return mm

                after(pe, l, "act", "ketok")
                mark("pe", heads_out(2, gv_tok, lambda h: s0_a[h * 32:h * 32 + 32, :],
                                     lambda h: q_s[h * 32:h * 32 + 32, 0, :], 32), "gla_o")
                after(pe, l, "dve", "gla_state")
                after(pe, l, "act", "gla_sq")
                for j in range(2):
                    mm = pe.matmul(ps_m[:, j, 0:T], C("mean64"), sq[j][:, :], start=True, stop=True)
                mark("pe", mm, "gla_ms")
                after(pe, l, "dve", "gla_o")
                after(pe, l, "dve", "gla_var")
                for i, (h, b) in enumerate(ATT):
                    n = KEYS[b] * P
                    if i:
                        after(pe, l, "dve", f"att_max{i - 1}")
                    for m in range(2):
                        r = slice(64 * m, 64 * m + 64)
                        q = z[r, DQ + h, TOK[b]:TOK[b] + P]
                        if b < 2:
                            mm = pe.matmul(ps_m[:, m, 0:n], q, z[r, DKK + h, 0:n], start=True, stop=True)
                        else:
                            pe.matmul(ps_m[:, m, 0:PAST], q, kc_t[r, h, :], start=True, stop=False, skip_group_check=True)
                            mm = pe.matmul(ps_m[:, m, PAST:n], q, z[r, DKK + h, TOK[2]:TOK[2] + P], start=False, stop=True,
                                           skip_group_check=True)
                    mark("pe", mm, f"att_s{i}")
                    after(pe, l, "dve", f"att_a{i}")
                    if i:
                        after(pe, l, "act", f"att_t{i - 1}")
                    for kt in range(KEYS[b]):
                        mm = pe.transpose(ps_m[:, 2, kt * P:(kt + 1) * P], probs[:, i % 2, 0, kt * P:(kt + 1) * P], C("ident"))
                    mark("pe", mm, f"att_t{i}")
                    after(pe, l, "act", f"att_t{i}")
                    if b == 0 and h:
                        after(pe, l, "act", f"att_o{i - 1}")
                    for kt in range(KEYS[b]):
                        v = (dv_tok[:, kt, h, :] if b < 2 else vc[:, kt, h * P:(h + 1) * P] if kt < 2 else dv_tok[:, 2, h, :])
                        o, a = (ps_m[:, 3, b * P:(b + 1) * P], probs_t[:, kt, :]) if b < 2 else \
                               (ps_m[:, 3, 256:320], probs_t[:, kt, 64:128])
                        mm = pe.matmul(o, v, a, start=b == 0 and kt == 0, stop=kt == KEYS[b] - 1, skip_group_check=True)
                    mark("pe", mm, f"att_o{i}")
                for h in range(H):
                    after(pe, l, "act", f"att_sq{h}")
                    if h >= 2:
                        after(pe, l, "dve", f"att_var{h - 2}")
                    mark("pe", pe.matmul(ps_m[:, h % 2, 0:T], C("mean128"), sq[h % 2][:, :], start=True, stop=True), f"att_ms{h}")
                after(pe, l, "act", "att_o11")
                for j in range(4):
                    if j >= 2:
                        after(pe, l, "dve", f"rot{j - 2}")
                    mark("pe", pe.matmul(ps_m[:, 2 + j % 2, 0:T], C("rot"), z[:, RQ + j, :], start=True, stop=True), f"rot{j}")
                after(pe, l, "dve", "rot3")
                after(pe, l, "dve", "att_var3")
                for h in range(H):
                    r = slice(64 * (h % 2), 64 * (h % 2) + 64)
                    q, k = z[r, RQ + h // 2, :], z[r, RK + h // 2, :]
                    bank = ps_m[:, h, :]
                    pe.matmul(bank[:, 256:512], k[:, 0:P], q[:, 0:256], start=True, stop=False, skip_group_check=True)
                    pe.matmul(bank[:, 0:128], k[:, P:2 * P], q[:, P:2 * P], start=False, stop=False, skip_group_check=True)
                    mm = pe.matmul(bank[:, 128:256], k[:, TOK[2]:T], q[:, TOK[2]:T], start=False, stop=True, skip_group_check=True)
                    mark("pe", mm, f"ret_s{h}")
                after(pe, l, "dve", "ret_k")
                for j in range(2):
                    for i in range(3):
                        mm = pe.transpose(ps_m[:, j, i * P:(i + 1) * P], (k_w, wgt)[j][:, TOK[i]:TOK[i] + P], C("ident"))
                    mark("pe", mm, f"ret_kt{j}")
                after(pe, l, "act", "ret_kt1")
                for j in range(2):
                    c = slice(j * P, (j + 1) * P)
                    for n in range(2):
                        pe.matmul(ps_m[:, j, 0:P], rk_tok[:, n, c], rv_tok[:, n, c], start=n == 0, stop=n == 1)
                    mm = pe.matmul(ps_m[:, j, P:2 * P], rk_tok[64:128, 2, c], rv_tok[64:128, 2, c], start=True, stop=True,
                                   skip_group_check=True)
                mark("pe", mm, "ret_state")
                mm = heads_out(2, rv_tok, lambda h: s0_r[64 * (h % 2):64 * (h % 2) + 64, h // 2, :],
                               lambda h: q_s[64 * (h % 2):64 * (h % 2) + 64, h // 2, :], 64)
                mark("pe", mm, "ret_o")
                after(pe, l, "dve", "ret_state")
                after(pe, l, "dve", "ret_o")
                for j in range(2):
                    mm = pe.matmul(ps_m[:, j, 0:T], C("mean64"), y[:, 6 + j, :], start=True, stop=True)
                mark("pe", mm, "ret_mu")
                after(pe, l, "act", "ret_sq")
                for j in range(2):
                    mm = pe.matmul(ps_m[:, 2 + j, 0:T], C("mean64"), sq[j][:, :], start=True, stop=True)
                mark("pe", mm, "ret_ms")
                unit_of_two(l, U_OUT, G_OUT, 0, xn_ready(l, 2), k_major=True)
                unit_of_two(l, U_OUT + 1, G_OUT + 1, 1, k_major=True)
                for s in range(2):
                    unit_of_two(l, U_OUT + 2 + s, G_OUT + 2 + s, s, k_major=True)
                sum_squares(l, 3)
                ffn(l, U_F2, G_F2, 4, 3)

            pe.wait_ge(x_new, (6 * DEPTH // 2 + 1) * KD)
            for n in range(3 * 2):
                if n >= 2:
                    pe.wait_ge(y_rows, n - 1)
                for q in range(4):
                    k = 4 * (n % 2) + q
                    i = n // 2
                    mm = pe.transpose(ps_m[:, n % 2, q * P:(q + 1) * P], x[:, k, TOK[i]:TOK[i] + P], C("ident"))
                mm.then_inc(y_mm, 1)

        def hi_of_unit(act, l, u, s, landed, cols):
            act.wait_ge(raw_in[s], l * RAW_LAYER + landed)
            act.wait_ge(w_used, l * UNITS + u + 1)
            act.activation(w_h[s][:, 0:cols], raw[s][:, 0:cols], ACT.Copy).then_inc(w_hi, 1)

        def lo_of_unit(dve, l, u, s, cols):
            dve.wait_ge(w_hi, l * UNITS + u + 1)
            dve.tensor_tensor(w_l[s][:, 0:cols], raw[s][:, 0:cols], w_h[s][:, 0:cols], ALU.subtract).then_inc(w_lo, 1)

        def unit_cols(u):
            down = N_UP <= u < U_MIX or u >= U_F2 + N_UP
            return HALF_DOWN * P if down else KD * P if u == U_MIX else 2 * KD * P

        def hi(act, l, u):
            hi_of_unit(act, l, u, u % 2, raw_after(u), unit_cols(u))

        def lo(dve, l, u):
            lo_of_unit(dve, l, u, u % 2, unit_cols(u))

        @block.scalar
        def _(act):
            act.dma_start(x_in[:, 0:2, :], ins["x_prompt"][0].rearrange("(i p) c -> p i c", p=P)).then_inc(x_loaded, 16)
            act.dma_start(x_in[0:64, 2, :], ins["x_prompt"][0, TOK[2]:T_P, :]).then_inc(x_loaded, 16)
            act.dma_start(x_in[64:128, 2, :], ins["x_sample"][0]).then_inc(x_loaded, 16)
            act.wait_ge(lam_s, 1)
            act.activation(lam_e[:, :], lam_e[:, :], ACT.Exp).then_inc(lam_s, 1)

            def split_hi(l, n, src, gain, first):
                for k in range(KD):
                    if first is not None:
                        act.wait_ge(x_new, l * 3 * KD + (first * KD + k + 1))
                    scale = 1.0 if gain is None else gain_l[:, gain, k:k + 1]
                    act.activation(xn_h[:, k, :], src[:, k, :], ACT.Copy, scale=scale).then_inc(xn_hi, 1)

            def squares():
                act.activation(rearr(y), rearr(x), ACT.Square).then_inc(sq_x, 1)

            def root(l, n):
                act.wait_ge(ss_var, l * 6 + n + 1)
                act.activation(var[:, :], var[:, :], ACT.Sqrt).then_inc(ss_sqrt, 1)

            def y_tile(l, m, acc, bank, b, gain, used, last):
                if used is not None:
                    act.wait_ge(w_used, used)
                act.wait_ge(y_acc, acc + 1)
                act.activation(sq[b][:, :], ps_g[:, bank, 0:T], ACT.Square).then_inc(y_sq, 1)
                i = act.activation(y_at(m), ps_g[:, bank, 0:T], ACT.Copy, scale=gain_l[:, gain, m:m + 1] if isinstance(m, int)
                                   else gain_l[:, gain, bass.ds(m, 1)])
                if last:
                    i.then_inc(evac, 1)

            def y_at(m):
                return y[:, m, :] if isinstance(m, int) else y[:, bass.ds(m, 1), :].rearrange("p a t -> p (a t)")

            def ffn(l, u0, norm, n, first, following):
                split_hi(l, n, x, norm, first)
                squares()
                root(l, norm)

                def up_step(l, v, s, used, landed, cols):
                    hi_of_unit(act, l, v + (u0 + 2) if not isinstance(v, int) else v + u0 + 2, s, landed, cols)
                    act.wait_ge(up_mul, l * 2 * KF + (v + (KF * (norm // 4) + 1)))
                    act.activation(gate[s][:, :], gate[s][:, :], ACT.Silu).then_inc(silu, 1)
                    act.wait_ge(prod, l * 2 * KF + (v + (KF * (norm // 4) + 1)))
                    i = act.activation(hid_h[:, bass.ds(v, 1), :].rearrange("p a t -> p (a t)") if not isinstance(v, int)
                                       else hid_h[:, v, :], up[s][:, :], ACT.Copy)
                    i.then_inc(hid_hi, 1)

                with act.Fori(0, N_UP // 2 - 1) as j:
                    for s in range(2):
                        up_step(l, 2 * j + s, s, None, 32 * j + raw_after(u0 + 2 + s), 2 * KD * P)
                for s in range(2):
                    up_step(l, N_UP - 2 + s, s, None, raw_after(u0 + N_UP + s), HALF_DOWN * P)
                d0 = u0 + N_UP
                acc0 = {0: 0, 4: 2 * KD}[norm]

                def down_tile(l, m, b, last_tile):
                    used = l * UNITS + (2 * m + (d0 + 2 + 2))
                    if not last_tile:
                        hi_of_unit(act, l, 2 * m + (d0 + 2), 0, 16 * m + raw_after(d0 + 2), HALF_DOWN * P)
                        y_tile(l, m, l * 3 * KD + (m + acc0) + (0 if b else 0), 2 * b, b, norm + 1, used, True)
                        hi_of_unit(act, l, 2 * m + (d0 + 3), 1, 16 * m + raw_after(d0 + 3), HALF_DOWN * P)
                    else:
                        y_tile(l, m, l * 3 * KD + (m + acc0), 2 * b, b, norm + 1, used, True)
                        if following is not None:
                            hi(act, l, following)
                            hi(act, l, following + 1)

                with act.Fori(0, KD // 2 - 1) as j:
                    for b in range(2):
                        down_tile(l, 2 * j + b, b, False)
                down_tile(l, KD - 2, 0, False)
                down_tile(l, KD - 1, 1, True)
                root(l, norm + 1)

            with act.Fori(0, DEPTH) as l:
                hi(act, l, 0)
                hi(act, l, 1)
                act.wait_ge(params, l + 1)
                ffn(l, U_F1, 0, 0, 0, U_MIX)
                split_hi(l, 1, x, 2, 1)
                squares()
                root(l, 2)
                for v in range(N_MIX):
                    hi(act, l, U_MIX + v + 2)
                act.wait_ge(evac, l * GROUPS + (G_MIX + N_MIX + 2))
                for i in range(2):
                    after(act, l, "pe", f"kct{i}")
                    mark("act", act.activation(kc_t[:, :, i * P:(i + 1) * P], ps_m[:, i, :].rearrange("p (h c) -> p h c", h=H),
                                               ACT.Copy), f"kct{i}")
                for n, (tile, at) in enumerate(SPLITS):
                    dst = dk_tok[:, :, at, :] if n < 4 else dv_tok[:, :, at, :] if n < 8 else \
                        (gv_tok if n < 10 else rv_tok)[:, :, at * P:(at + 1) * P]
                    after(act, l, "pe", f"tok{n}")
                    mark("act", act.activation(dst, ps_m[:, 2 + n % 2, 0:3 * P].rearrange("p (i c) -> p i c", i=3), ACT.Copy),
                         f"tok{n}")
                after(act, l, "pe", "logit")
                mark("act", act.activation(wgt[:, :], ps_m[:, 0, 0:T], ACT.Abs, bias=small_l[:, 0:1]), "abs")
                act.drain()
                act.activation(wgt[:, :], wgt[:, :], ACT.Exp, scale=-1.0)
                act.drain()
                mark("act", act.activation(wgt[:, :], wgt[:, :], ACT.Ln, bias=1.0), "softplus")
                for n, c in enumerate(LEVELS[:-1]):
                    cols = slice(0, T_P if c >= 64 else T)
                    after(act, l, "dve", f"dist{n}")
                    act.activation(wgt[:, cols], wgt[:, cols], ACT.Abs)
                    act.drain()
                    mark("act", act.activation(wgt[:, cols], wgt[:, cols], ACT.Exp, scale=-1.0 / 16), f"weight{n}")
                mark("act", act.activation(q_s[:, 0, :], decay[:, T_P:T], ACT.Exp, scale=1.0 / 16), "from_start")
                after(act, l, "dve", "qk7")
                for n, t in enumerate((T_P - 1, T - 1)):
                    act.activation(tiny[:, n:n + 1], decay[:, t:t + 1], ACT.Copy, scale=1.0 / 16)
                    act.activation(tiny[:, 2 + n:3 + n], decay[:, t:t + 1], ACT.Exp, scale=1.0 / 16)
                act.drain()
                act.activation(wgt[:, 0:T_P], decay[:, 0:T_P], ACT.Exp, scale=-1.0 / 16, bias=tiny[:, 0:1])
                mark("act", act.activation(wgt[:, T_P:T], decay[:, T_P:T], ACT.Exp, scale=-1.0 / 16, bias=tiny[:, 1:2]), "to_end")
                after(act, l, "pe", "ketok")
                mark("act", act.activation(gk_tok[:, :, :], ps_m[:, 2, 0:3 * P].rearrange("p (i c) -> p i c", i=3), ACT.Copy),
                     "ketok")
                after(act, l, "dve", "gla_o")
                for j in range(2):
                    i = act.activation(sq[j][:, :], y[:, j, :], ACT.Square)
                mark("act", i, "gla_sq")
                after(act, l, "dve", "gla_var")
                for j, v in enumerate((q_w, k_w)):
                    i = act.activation(v[:, :], v[:, :], ACT.Sqrt)
                mark("act", i, "gla_sqrt")
                g = z[:, GR:GR + 2, :]
                mark("act", act.activation(g, g, ACT.Silu), "gla_gate")
                for i, (h, b) in enumerate(ATT):
                    n, s = KEYS[b] * P, i % 2
                    after(act, l, "dve", f"att_max{i}")
                    for m in range(2):
                        p = probs[:, s, m, 0:n]
                        e = act.activation(p, p, ACT.Exp, bias=tiny[:, 8 + 2 * s + m:9 + 2 * s + m],
                                           accum_out=tiny[:, 12 + 2 * s + m:13 + 2 * s + m])
                    mark("act", e, f"att_e{i}")
                    after(act, l, "pe", f"att_t{i}")
                    mark("act", act.activation(probs_t[:, 0:KEYS[b], :], ps_m[:, 2, 0:n].rearrange("p (k c) -> p k c", c=P), ACT.Copy),
                         f"att_t{i}")
                    if b == 2:
                        after(act, l, "pe", f"att_o{i}")
                        mark("act", act.activation(y[:, 2 + h, :], ps_m[:, 3, 0:T], ACT.Copy), f"att_o{i}")
                act.drain()
                for h in range(H):
                    if h >= 2:
                        after(act, l, "pe", f"att_ms{h - 2}")
                    mark("act", act.activation(sq[h % 2][:, :], y[:, 2 + h, :], ACT.Square), f"att_sq{h}")
                    after(act, l, "dve", f"att_var{h}")
                    v = (q_w, k_w)[h % 2]
                    mark("act", act.activation(v[:, :], v[:, :], ACT.Sqrt), f"att_sqrt{h}")
                for j in range(2):
                    after(act, l, "pe", f"ret_kt{j}")
                    mark("act", act.activation(rk_tok[:, :, j * P:(j + 1) * P],
                                               ps_m[:, j, 0:3 * P].rearrange("p (i c) -> p i c", i=3), ACT.Copy), f"ret_kt{j}")
                after(act, l, "dve", "ret_xc")
                for j in range(2):
                    i = act.activation(sq[j][:, :], y[:, 6 + j, :], ACT.Square)
                mark("act", i, "ret_sq")
                after(act, l, "dve", "ret_var")
                for j, v in enumerate((q_w, k_w)):
                    i = act.activation(v[:, :], v[:, :], ACT.Sqrt)
                mark("act", i, "ret_sqrt")
                g = z[:, RG:RG + 2, :]
                mark("act", act.activation(g, g, ACT.Silu), "ret_gate")
                act.wait_ge(kv_stored, (l + 1) * 64)
                after(act, l, "dve", "ret_done")
                split_hi(l, 2, y, None, None)
                for v in range(N_OUT):
                    s = v % 2
                    for n in range(2):
                        m = 2 * v + n
                        if v or n:
                            acc = l * 3 * KD + (KD + max(m - 1, 0))
                        else:
                            acc = l * 3 * KD + KD
                        y_tile(l, m, acc, 2 * s + n, n, 3, l * UNITS + (U_OUT + v + 3) if n == 0 else None, n == 1)
                    hi(act, l, U_OUT + v + 2)
                root(l, 3)
                act.wait_ge(st_stored, (l + 1) * 64)
                ffn(l, U_F2, 4, 3, 2, None)

            for i in range(3):
                n = 2 * i + 1
                act.wait_ge(y_rows, n + 1)
                if i < 2:
                    act.dma_start(outs["y_prompt"][0, i * P:(i + 1) * P, :], x_in[:, i, :]).then_inc(y_stored, 16)
                else:
                    act.dma_start(outs["y_sample"][0], x_in[64:128, i, :]).then_inc(y_stored, 16)
            act.wait_ge(y_stored, 48)

        @block.vector
        def _(dve):
            dve.sem_inc(w_lo, 2)
            dve.sem_inc(evac, 2)
            dve.sem_inc(y_acc, 1)
            dve.wait_ge(loaded, N_LOADED)
            dve.tensor_copy(mask[:, :, :].rearrange("p a b -> p (a b)"), mask_in[:, :])
            lam_v = lam_in[:, :, :, :].rearrange("p l (a b) d -> p (l a) b d", b=2)
            dve.tensor_tensor(lam_p[:, :, :], lam_v[:, :, 0, :], lam_v[:, :, 1, :], ALU.mult)
            dve.drain()
            dve.tensor_reduce(lam_e[:, :], lam_p[:, :, :], axis=AX.X, op=ALU.add).then_inc(lam_s, 1)
            for k in range(KD):
                dve.wait_ge(x_mm, k + 1)
                dve.tensor_copy(x[:, k, :], ps_m[:, k % 2, 0:T]).then_inc(x_new, 1)
            dve.wait_ge(lam_s, 2)
            lam_v2 = lam_e[:, :].rearrange("p (l a) -> p l a", a=2)
            dve.tensor_tensor(lam_all[:, :], lam_v2[:, :, 0], lam_v2[:, :, 1], ALU.subtract)
            dve.drain()
            dve.tensor_tensor(lam_all[:, :], lam_all[:, :], C("lam")[:, 0:DEPTH], ALU.add)
            for l in range(DEPTH):
                dve.tensor_scalar(small[:, l, 7:8], small[:, l, 3:4], C("lam")[:, DEPTH + l:DEPTH + l + 1], None, ALU.mult)
            dve.drain()
            for l in range(DEPTH):
                dve.tensor_copy(small[:, l, 6:7], lam_all[:, l:l + 1])
            dve.drain()

            def split_lo(l, n, k, src, gain):
                dve.wait_ge(xn_hi, l * 32 + (8 * n + k + 1))
                if gain is None:
                    i = dve.tensor_tensor(xn_l[:, k, :], src[:, k, :], xn_h[:, k, :], ALU.subtract)
                else:
                    i = dve.scalar_tensor_tensor(xn_l[:, k, :], src[:, k, :], gain_l[:, gain, k:k + 1], xn_h[:, k, :],
                                                 ALU.mult, ALU.subtract)
                i.then_inc(xn_lo, 1)

            def root(l, n, half=False):
                c = 4.0 if half else 1.0
                dve.wait_ge(ss_mm, l * 6 + n + 1)
                dve.tensor_scalar(var[:, :], ps_m[:, 0, 0:T], c / D, c * EPS, ALU.mult, ALU.add).then_inc(ss_var, 1)
                dve.wait_ge(ss_sqrt, l * 6 + n + 1)
                dve.reciprocal(rs[:, :], var[:, :])
                dve.drain()

            def pre(l, n, norm, sq_n, update):
                for k in range(KD + 1):
                    if k < KD and update:
                        dve.tensor_tensor(y[:, k, :], y[:, k, :], rs[:, :], ALU.mult)
                        dve.drain()
                        dve.tensor_tensor(x[:, k, :], x[:, k, :], y[:, k, :], ALU.add).then_inc(x_new, 1)
                    if k and norm is not None:
                        if k == 1:
                            dve.drain()
                        split_lo(l, n, k - 1, x, norm)
                if norm is None:
                    return
                dve.wait_ge(sq_x, l * 3 + (sq_n + 1))
                dve.tensor_reduce(ssum[:, :], y[:, :, :].rearrange("p k t -> p t k"), axis=AX.X, op=ALU.add).then_inc(ss_in, 1)

            def ffn(l, u0, g0, norm, following):
                f = norm // 4

                def up_step(l, v, s, cols):
                    dve.wait_ge(w_used, l * UNITS + (v + (u0 + 3)))
                    dve.tensor_tensor(gate[s][:, :], ps_g[:, 2 * s, 0:T], rs[:, :], ALU.mult).then_inc(up_mul, 1)
                    dve.tensor_tensor(up[s][:, :], ps_g[:, 2 * s + 1, 0:T], rs[:, :], ALU.mult).then_inc(evac, 1)
                    lo_of_unit(dve, l, v + (u0 + 2), s, cols)
                    dve.drain()
                    dve.wait_ge(silu, l * 2 * KF + (v + (KF * f + 1)))
                    dve.tensor_tensor(up[s][:, :], up[s][:, :], gate[s][:, :], ALU.mult).then_inc(prod, 1)
                    dve.wait_ge(hid_hi, l * 2 * KF + (v + (KF * f + 1)))
                    at = (lambda t: t[:, v, :]) if isinstance(v, int) else \
                        (lambda t: t[:, bass.ds(v, 1), :].rearrange("p a t -> p (a t)"))
                    dve.tensor_tensor(at(hid_l), up[s][:, :], at(hid_h), ALU.subtract).then_inc(hid_lo, 1)

                with dve.Fori(0, N_UP // 2 - 1) as j:
                    for s in range(2):
                        up_step(l, 2 * j + s, s, 2 * KD * P)
                for s in range(2):
                    up_step(l, N_UP - 2 + s, s, HALF_DOWN * P)
                dve.memset(ssum[:, :], 0.0)
                acc0 = {0: 0, 4: 2 * KD}[norm]
                d0 = u0 + N_UP

                def down_tile(l, m, b, last):
                    if not last:
                        lo_of_unit(dve, l, 2 * m + (d0 + 2), 0, HALF_DOWN * P)
                    add_square(l * 3 * KD + (m + (acc0 + 1)), b, last)
                    if not last:
                        lo_of_unit(dve, l, 2 * m + (d0 + 3), 1, HALF_DOWN * P)
                    elif following is not None:
                        lo(dve, l, following)
                        lo(dve, l, following + 1)

                with dve.Fori(0, KD // 2 - 1) as j:
                    for b in range(2):
                        down_tile(l, 2 * j + b, b, False)
                down_tile(l, KD - 2, 0, False)
                down_tile(l, KD - 1, 1, True)
                dve.wait_ge(evac, l * GROUPS + (g0 + N_UP + KD + 2))
                root(l, norm + 1, half=True)

            def add_square(count, b, last):
                dve.drain()
                dve.wait_ge(y_sq, count)
                dve.tensor_tensor(ssum[:, :], ssum[:, :], sq[b][:, :], ALU.add).then_inc(y_acc, 1)
                if last:
                    dve.drain()
                    dve.sem_inc(ss_in, 1)

            def head_norm(tile, v, gain):
                dve.reciprocal(v[:, :], v[:, :])
                dve.drain()
                return dve.scalar_tensor_tensor(y[:, tile, :], y[:, tile, :], gain, v[:, :], ALU.mult, ALU.mult)

            with dve.Fori(0, DEPTH) as l:
                dve.tensor_copy(gain_l[:, :, :].rearrange("p a k -> p (a k)"),
                                gains[:, bass.ds(l, 1), :, :].rearrange("p o a k -> p (o a k)"))
                dve.tensor_copy(small_l[:, :], small[:, bass.ds(l, 1), :].rearrange("p o a -> p (o a)"))
                dve.tensor_copy(a2_l[:, :], a2[:, bass.ds(l, 1), :].rearrange("p o a -> p (o a)")).then_inc(params, 1)
                dve.drain()
                lo(dve, l, 0)
                lo(dve, l, 1)
                pre(l, 0, 0, 0, False)
                root(l, 0)
                ffn(l, U_F1, G_F1, 0, U_MIX)
                pre(l, 1, 2, 1, True)
                root(l, 2)
                dve.wait_ge(w_used, l * UNITS + (U_MIX + 3))
                dve.tensor_tensor(alr[0:RANK, :], ps_g[0:RANK, 0, 0:T], rs[0:RANK, :], ALU.mult).then_inc(evac, 1)
                lo(dve, l, U_MIX + 2)
                rs2 = rs[:, :].rearrange("p (o t) -> p o t", o=1).broadcast_to([P, 2, T])
                for v in range(1, N_MIX):
                    s = v % 2
                    dve.wait_ge(w_used, l * UNITS + (U_MIX + v + 3))
                    dve.tensor_tensor(z[:, 2 * v - 2:2 * v, :], ps_g[:, 2 * s:2 * s + 2, 0:T], rs2, ALU.mult).then_inc(evac, 1)
                    lo(dve, l, U_MIX + v + 2)
                dve.drain()
                after(dve, l, "pe", "logit")
                after(dve, l, "act", "abs")
                dve.tensor_scalar(z[:, GQ, :], z[:, GQ, :], DK_A ** -0.5, None, ALU.mult)
                mark("dve", dve.tensor_scalar(q_w[:, :], ps_m[:, 0, 0:T], small_l[:, 0:1], 0.0, ALU.add, ALU.min), "minus")
                dve.drain()
                after(dve, l, "act", "softplus")
                dve.tensor_tensor(k_w[:, :], q_w[:, :], wgt[:, :], ALU.subtract)
                dve.drain()
                one = C("ones_row")
                dve.tensor_tensor_scan(decay[:, 0:T_P], one[:, 0:T_P], k_w[:, 0:T_P], 0.0, ALU.mult, ALU.add)
                mark("dve", dve.tensor_tensor_scan(decay[:, T_P:T], one[:, 0:T_S], k_w[:, T_P:T], 0.0, ALU.mult, ALU.add), "decay")
                dve.wait_ge(mem_set, l + 1)
                then_pass(dve)
                for n, c in enumerate(LEVELS):
                    if c:
                        cols = slice(0, T_P if c >= 64 else T)
                        dve.drain()
                        if c == 128:
                            i = dve.tensor_scalar(wgt[:, cols], decay[:, cols], decay[:, 127:128], None, ALU.subtract)
                        else:
                            v = decay[:, cols].rearrange("p (b c) -> p b c", c=2 * c)
                            nb = v.shape[1]
                            i = dve.tensor_tensor(wgt[:, cols].rearrange("p (b c) -> p b c", c=2 * c), v,
                                                  v[:, :, c - 1:c].broadcast_to([P, nb, 2 * c]), ALU.subtract)
                        mark("dve", i, f"dist{n}")
                        after(dve, l, "act", f"weight{n}")
                        if n:
                            after(dve, l, "pe", f"level{n - 1}")
                        dve.tensor_tensor(q_w[:, cols], z[:, GQ, cols], wgt[:, cols], ALU.mult)
                        mark("dve", dve.tensor_tensor(k_w[:, cols], z[:, GK, cols], wgt[:, cols], ALU.mult), f"qk{n}")
                    after(dve, l, "pe", f"level{n}")
                    if n == 0:
                        i = dve.tensor_copy(scores[:, :, 3, :], ps_m[:, :, 3 * P:4 * P])
                    else:
                        then_pass(dve)
                        for a, b in (((0, P), (2 * P, 3 * P)) if n == 1 else ((0, 3 * P),)):
                            m = mask[:, n - 1:n, a:b].broadcast_to([P, H, b - a])
                            i = dve.copy_predicated(scores[:, :, :, :].rearrange("p h b c -> p h (b c)")[:, :, a:b], m,
                                                    ps_m[:, :, a:b])
                        dve.drain()
                    mark("dve", i, f"score{n}")
                after(dve, l, "act", "from_start")
                mark("dve", dve.tensor_tensor(q_s[:, 0, :], q_s[:, 0, :], z[:, GQ, T_P:T], ALU.mult), "q_start")
                after(dve, l, "act", "to_end")
                mark("dve", dve.tensor_tensor(k_w[:, :], z[:, GK, :], wgt[:, :], ALU.mult), "k_end")
                after(dve, l, "pe", "gla_state")
                dve.wait_ge(past_in, (l + 1) * 64)
                for h in range(H):
                    r, c = slice(32 * h, 32 * h + 32), slice(64 * h, 64 * h + 64)
                    dve.tensor_copy(st_a[r, 0, :], ps_m[r, 0, c])
                    i = dve.scalar_tensor_tensor(st_a[r, 1, :], s0_a[r, :], tiny[r, 3:4], ps_m[r, 1, c], ALU.mult, ALU.add)
                mark("dve", i, "gla_state")
                after(dve, l, "pe", "gla_o")
                mark("dve", dve.tensor_copy(y[:, 0:2, :], ps_m[:, 2:4, 0:T]), "gla_o")
                after(dve, l, "pe", "gla_ms")
                for j, v in enumerate((q_w, k_w)):
                    i = dve.tensor_scalar(v[:, :], ps_m[:, j, 0:T], EPS, None, ALU.add)
                mark("dve", i, "gla_var")
                after(dve, l, "act", "gla_gate")
                for j, v in enumerate((q_w, k_w)):
                    head_norm(j, v, small_l[:, 1 + j:2 + j])
                dve.drain()
                mark("dve", dve.tensor_tensor(y[:, 0:2, :], y[:, 0:2, :], z[:, GR:GR + 2, :], ALU.mult), "gla_done")
                for i, (h, b) in enumerate(ATT):
                    n, s = KEYS[b] * P, i % 2
                    pr = probs[:, s, :, 0:n]
                    bias = C(f"bias{h}")[:, BIAS_AT[b]:BIAS_AT[b] + n].rearrange("p (o c) -> p o c", o=1).broadcast_to([P, 2, n])
                    after(dve, l, "pe", f"att_s{i}")
                    if i >= 2:
                        after(dve, l, "pe", f"att_t{i - 2}")
                    dve.scalar_tensor_tensor(pr, ps_m[:, 0:2, 0:n], DK_D ** -0.5, bias, ALU.mult, ALU.add)
                    dve.drain()
                    mark("dve", dve.tensor_reduce(tiny[:, 8 + 2 * s:10 + 2 * s], pr, axis=AX.X, op=ALU.max, negate=True), f"att_max{i}")
                    after(dve, l, "act", f"att_e{i}")
                    inv = tiny[:, 16 + 2 * s:18 + 2 * s]
                    dve.reciprocal(inv, tiny[:, 12 + 2 * s:14 + 2 * s])
                    dve.drain()
                    dve.tensor_scalar(probs[:, s, 1, 0:n], probs[:, s, 1, 0:n], inv[:, 1:2], small_l[:, 6:7], ALU.mult, ALU.mult)
                    dve.drain()
                    mark("dve", dve.scalar_tensor_tensor(probs[:, s, 0, 0:n], probs[:, s, 0, 0:n], inv[:, 0:1], probs[:, s, 1, 0:n],
                                                         ALU.mult, ALU.subtract), f"att_a{i}")
                for h in range(H):
                    v = (q_w, k_w)[h % 2]
                    after(dve, l, "pe", f"att_ms{h}")
                    mark("dve", dve.tensor_scalar(v[:, :], ps_m[:, h % 2, 0:T], EPS, None, ALU.add), f"att_var{h}")
                    after(dve, l, "act", f"att_sqrt{h}")
                    mark("dve", head_norm(2 + h, v, small_l[:, 7:8]), f"att_done{h}")
                for j in range(4):
                    dve.drain()
                    after(dve, l, "pe", f"rot{j}")
                    c = 1.0 if j < 2 else DK_R ** -0.5
                    zt = z[:, RQ + j, :]
                    dve.scalar_tensor_tensor(wgt[:, :], ps_m[:, 2 + j % 2, 0:T], c, C("sin"), ALU.mult, ALU.mult)
                    dve.scalar_tensor_tensor(zt, zt, c, C("cos"), ALU.mult, ALU.mult)
                    dve.drain()
                    mark("dve", dve.tensor_tensor(zt, zt, wgt[:, :], ALU.add), f"rot{j}")
                for h in range(H):
                    after(dve, l, "pe", f"ret_s{h}")
                    mark("dve", dve.tensor_tensor(scores[:, h, :, :].rearrange("p b c -> p (b c)"), ps_m[:, h, :], C(f"dec{h}"), ALU.mult),
                         f"ret_s{h}")
                dve.drain()
                for j in range(2):
                    i = dve.tensor_tensor(q_s[:, j, :], z[:, RQ + j, T_P:T], C(f"q_dec{j}"), ALU.mult)
                mark("dve", i, "ret_q")
                for j, t in enumerate((k_w, wgt)):
                    i = dve.tensor_tensor(t[:, :], z[:, RK + j, :], C(f"k_dec{j}"), ALU.mult)
                mark("dve", i, "ret_k")
                after(dve, l, "pe", "ret_state")
                for j in range(2):
                    for hh in range(2):
                        r = slice(64 * hh, 64 * hh + 64)
                        g = float((1.0 - 2.0 ** (-5.0 - (2 * j + hh))) ** T_S)
                        dve.tensor_copy(st_r[r, 0, j, :], ps_m[r, j, 64 * hh:64 * hh + 64])
                        i = dve.scalar_tensor_tensor(st_r[r, 1, j, :], s0_r[r, j, :], g, ps_m[r, j, P + 64 * hh:P + 64 * hh + 64],
                                                     ALU.mult, ALU.add)
                mark("dve", i, "ret_state")
                after(dve, l, "pe", "ret_o")
                mark("dve", dve.tensor_copy(y[:, 6:8, :], ps_m[:, 2:4, 0:T]), "ret_o")
                dve.drain()
                after(dve, l, "pe", "ret_mu")
                mark("dve", dve.tensor_tensor(y[:, 6:8, :], y[:, 6:8, :], ps_m[:, 0:2, 0:T], ALU.subtract), "ret_xc")
                after(dve, l, "pe", "ret_ms")
                for j, v in enumerate((q_w, k_w)):
                    i = dve.tensor_scalar(v[:, :], ps_m[:, 2 + j, 0:T], EPS, None, ALU.add)
                mark("dve", i, "ret_var")
                after(dve, l, "act", "ret_gate")
                for j, v in enumerate((q_w, k_w)):
                    head_norm(6 + j, v, small_l[:, 4 + j:5 + j])
                dve.drain()
                mark("dve", dve.tensor_tensor(y[:, 6:8, :], y[:, 6:8, :], z[:, RG:RG + 2, :], ALU.mult), "ret_done")
                dve.drain()
                for k in range(KD):
                    split_lo(l, 2, k, y, None)
                dve.memset(ssum[:, :], 0.0)
                for v in range(N_OUT):
                    for n in range(2):
                        m = 2 * v + n
                        add_square(l * 3 * KD + (KD + m + 1), n, m == KD - 1)
                    lo(dve, l, U_OUT + v + 2)
                dve.wait_ge(evac, l * GROUPS + (G_OUT + N_OUT + 2))
                root(l, 3)
                pre(l, 3, 4, 2, True)
                dve.wait_ge(st_stored, (l + 1) * 64)
                root(l, 4)
                ffn(l, U_F2, G_F2, 4, None)
                pre(l, 0, None, 0, True)
                dve.drain()

            for n in range(6):
                i, half = n // 2, n % 2
                dve.wait_ge(y_mm, n + 1)
                dve.tensor_copy(x_in[:, i, half * 512:(half + 1) * 512], ps_m[:, half, :]).then_inc(y_rows, 1)

        for k, n in reached.items():
            assert n == len(MILESTONES[k]), (k, n, len(MILESTONES[k]))


_INS = ["x_prompt", "x_sample", "cache_diff_k", "cache_diff_v", "state_gla", "state_ret",
        "ffn1_norm_pre", "ffn1_w_up", "ffn1_w_down", "ffn1_norm_post", "mix_norm_pre", "w_in", "w_gla_a2", "b_gla_a",
        "gla_norm", "diff_lambda", "diff_subln", "ret_norm", "w_out", "mix_norm_post",
        "ffn2_norm_pre", "ffn2_w_up", "ffn2_w_down", "ffn2_norm_post"]
_OUTS = {
    "y_prompt": (1, T_P, D), "y_sample": (1, T_S, D),
    "new_k_prompt": (DEPTH, 1, T_P, H, 2 * DK_D), "new_v_prompt": (DEPTH, 1, T_P, H, DV_D),
    "state_gla_prompt": (DEPTH, 1, H, DK_A, DV_A), "state_ret_prompt": (DEPTH, 1, H, DK_R, DV_R),
    "new_k_sample": (DEPTH, 1, T_S, H, 2 * DK_D), "new_v_sample": (DEPTH, 1, T_S, H, DV_D),
    "state_gla_sample": (DEPTH, 1, H, DK_A, DV_A), "state_ret_sample": (DEPTH, 1, H, DK_R, DV_R),
}


def kernel(**inputs):
    import numpy as _np
    import concourse.bacc as _bacc
    from concourse import mybir as _mybir
    from concourse.bass_utils import run_bass_kernel_spmd as _run

    nc = _bacc.Bacc("TRN2", target_bir_lowering=False, num_devices=1)
    tables, table_at, masks = constants()
    arrays, ins, outs = {}, {}, {}
    for name in _INS + ["tables", "masks"]:
        a = _np.ascontiguousarray(tables if name == "tables" else masks if name == "masks" else inputs[name])
        arrays[f"in_{name}_dram"] = a
        ins[name] = nc.dram_tensor(f"in_{name}_dram", a.shape, _mybir.dt.from_np(a.dtype), kind="ExternalInput").ap()
    for name, shape in _OUTS.items():
        outs[name] = nc.dram_tensor(f"out_{name}_dram", shape, F32, kind="ExternalOutput").ap()
    build(nc, ins, outs, table_at)
    r = _run(nc, [arrays], core_ids=[0])
    return tuple(r.results[0][f"out_{name}_dram"] for name in _OUTS)
```

```python
from contextlib import ExitStack

import numpy as np
import concourse.bass as bass
from concourse import mybir

F32 = mybir.dt.float32
F32R = mybir.dt.float32r
U8 = mybir.dt.uint8
ACT = mybir.ActivationFunctionType
ALU = mybir.AluOpType
AX = mybir.AxisListType

P = 128
DEPTH, D, D_FF, D_IN = 2, 1024, 2816, 3344
T_P, T_S, PAST = 256, 64, 256
T = T_P + T_S
KD = D // P
KF = D_FF // P
TOK = (0, 128, 192)
EPS = 1e-6
RANK, H, DK_A, DV_A, DK_D, DV_D, DK_R, DV_R = 16, 4, 32, 64, 64, 128, 64, 64
C_BIAS, C_GLA, C_ATT, C_RET, C_LAM, C_ATT1 = 0, 1, 3, 4, 6, 7
PARAMS = 6 * KD + 8
ROWS = 6 * KD + 6
HALF_DOWN = KF // 2

N_UP, N_DOWN, N_MIX, N_OUT = KF, 2 * KD, 14, KD // 2
U_F1, U_MIX = 0, N_UP + N_DOWN
U_OUT = U_MIX + N_MIX
U_F2 = U_OUT + N_OUT
UNITS = U_F2 + N_UP + N_DOWN
G_F1, G_MIX = 0, N_UP + KD
G_OUT = G_MIX + N_MIX
G_F2 = G_OUT + N_OUT
GROUPS = G_F2 + N_UP + KD

GQ, GK, GV, GR, DQ, DKK, DV, RQ, RK, RV, RG = 0, 1, 2, 4, 6, 10, 14, 18, 20, 22, 24
NZ = 26
HEAD_AT = ((0, 2, "head64"), (2, 2, "head64"), (8, 1, "head128"), (9, 1, "head128"), (10, 1, "head128"), (11, 1, "head128"),
           (4, 2, "head64"), (6, 2, "head64"))
UNIT_TILE = (None, GQ, GV, DQ, DQ + 2, DKK, DKK + 2, DV, DV + 2, RQ, RK, RV, GR, RG)
HEAD_ORDER = (0, 1, 6, 7, 2, 3, 4, 5)
LEVELS = (128, 64, 32, 16, 8, 4, 2, 1, 0)
SPLITS = ((DKK, 0), (DKK + 1, 1), (DKK + 2, 2), (DKK + 3, 3), (DV, 0), (DV + 1, 1), (DV + 2, 2), (DV + 3, 3),
          (GV, 0), (GV + 1, 1), (RV, 0), (RV + 1, 1))
ATT = [(h, b) for h in range(H) for b in range(3)]
KEYS = (1, 2, 3)
BIAS_AT = (0, 128, 384)


HALVES = ((0, 4), (4, 8))
THIRDS = ((0, 3), (3, 6), (6, 8))
SCHEDULE = (
    [("part", 2, 0, 4), ("logit",), ("part", 2, 4, 8), ("past",), ("part", 3, 0, 4), ("tok", 8), ("tok", 9), ("part", 3, 4, 8)]
    + [x for n in range(9) for x in (("level", n), ("part", 4 + n // 2, *HALVES[n % 2]))]
    + [("gla_keys",), ("part", 8, 4, 8), ("gla_out",)]
    + [x for n, t in enumerate((4, 6, 0, 2)) for x in (("part", 9, 2 * n, 2 * n + 2), ("tok", t), ("tok", t + 1))]
    + [x for n in range(12) for x in (("part", 10 + n // 3, *THIRDS[n % 3]), ("att", n))
       + ((("rot", n - 4),) if 4 <= n < 8 else ()) + ((("ret_s", n - 8),) if n >= 8 else ())]
    + [("ret_keys",), ("att", 12), ("ret_out",), ("att", 13), ("norms",)]
)


def milestones():
    pe, act, dve, pool = [], [], [], []
    for kind, *arg in SCHEDULE:
        n = arg[0] if arg else None
        if kind == "past":
            pe += ["kct0", "kct1"]
            act += ["kct0", "kct1"]
        elif kind == "tok":
            pe.append(f"tok{n}")
            act.append(f"tok{n}")
        elif kind == "logit":
            pe.append("logit")
            act += ["abs", "softplus"]
            dve += ["minus", "decay"]
            pool.append("dist0")
        elif kind == "level":
            if n == 0:
                act.append("weight0")
                pool.append("qk0")
            if n < 7:
                pool.append(f"dist{n + 1}")
                act.append(f"weight{n + 1}")
                pool.append(f"qk{n + 1}")
            pe.append(f"level{n}")
            dve.append(f"score{n}")
        elif kind == "gla_keys":
            act += ["from_start", "to_end", "ketok"]
            dve += ["q_start", "k_end"]
            pe.append("ketok")
        elif kind == "gla_out":
            pe += ["gla_state", "gla_o"]
            dve += ["gla_state", "gla_o"]
        elif kind == "att":
            if n >= 2:
                pe.append(f"att_t{n - 2}")
                act.append(f"att_t{n - 2}")
            if n < 12:
                pe.append(f"att_s{n}")
                dve.append(f"att_max{n}")
                act.append(f"att_e{n}")
            if 1 <= n <= 12:
                dve.append(f"att_a{n - 1}")
            if n >= 2:
                pe.append(f"att_o{n - 2}")
                if n % 3 == 1:
                    act.append(f"att_o{n - 2}")
        elif kind == "rot":
            pe.append(f"rot{n}")
            dve.append(f"rot{n}")
        elif kind == "ret_s":
            pe.append(f"ret_s{n}")
            dve.append(f"ret_s{n}")
        elif kind == "ret_keys":
            dve += ["ret_q", "ret_k"]
            pe += ["tok10", "tok11", "ret_kt0", "ret_kt1"]
            act += ["gates", "tok10", "tok11", "ret_kt0", "ret_kt1"]
        elif kind == "ret_out":
            pe += ["ret_state", "ret_o", "ret_mu"]
            dve += ["ret_state", "ret_o", "ret_xc"]
        elif kind == "norms":
            act += ["squares", "sqrt"]
            pe += ["ms"] + [f"spread{q}" for q in HEAD_ORDER]
            dve += ["var", "inv"] + [f"head{q}" for q in HEAD_ORDER]
    return {"pe": pe, "act": act, "dve": dve, "pool": pool}


MILESTONES = milestones()


def constants():
    parts, at = [], {}

    def add(name, a):
        at[name] = (sum(x.shape[1] for x in parts), a.shape[1])
        parts.append(a.astype(np.float32))

    r = np.arange(P)
    add("ident", np.eye(P))
    add("ones", np.ones((P, 1)))
    lam = 0.8 - 0.6 * np.exp(-0.3 * np.arange(DEPTH))
    add("lam", np.tile(np.concatenate([lam, 1.0 - lam])[None, :], (P, 1)))
    add("mean64", np.kron(np.eye(2), np.ones((64, 64))) / 64.0)
    add("head64", np.kron(np.eye(2), np.ones((64, 1))) / 64.0)
    add("head128", np.ones((P, 1)) / 128.0)
    rot = np.zeros((P, P))
    for g in (0, 64):
        for i in range(32):
            rot[g + 32 + i, g + i] = -1.0
            rot[g + i, g + 32 + i] = 1.0
    add("rot", rot)
    pos = np.concatenate([np.arange(T_P), PAST + np.arange(T_S)]).astype(np.float32)
    inv = np.float32(10000.0) ** (-np.arange(32, dtype=np.float32) / np.float32(32))
    ang = pos[None, :] * inv[r % 32][:, None]
    add("cos", np.cos(ang.astype(np.float32)))
    add("sin", np.sin(ang.astype(np.float32)))
    lg = np.log(1.0 - 2.0 ** (-5.0 - np.arange(H)))
    loc = np.concatenate([np.arange(T_P), np.arange(T_S)])
    last = np.concatenate([np.full(T_P, T_P - 1), np.full(T_S, T_S - 1)])
    for j in range(2):
        add(f"k_dec{j}", np.exp((last - loc)[None, :] * lg[2 * j + r // 64][:, None]))
    for j in range(2):
        add(f"q_dec{j}", np.exp((np.arange(T_S) + 1.0)[None, :] * lg[2 * j + r // 64][:, None]))
    for h in range(H):
        dt = r[None, :] - r[:, None]
        diag = np.where(dt >= 0, np.exp(np.maximum(dt, 0) * lg[h]), 0.0)
        samp = np.where((r[:, None] >= 64) & (r[None, :] >= 64), diag, 0.0)
        add(f"dec{h}", np.concatenate([diag, samp, diag, np.exp((dt + 128) * lg[h])], axis=1))
    for h in range(H):
        slope = 2.0 ** (-8.0 * (h + 1) / H)

        def bias(qp, kp):
            b = -slope * np.abs(qp[:, None] - kp[None, :])
            return np.where(kp[None, :] // 64 <= qp[:, None] // 64, b, -1e30)

        b2 = bias(PAST + r % 64, np.concatenate([np.arange(PAST), PAST - 64 + r]))
        b2[:, PAST:PAST + 64] = -1e30
        add(f"bias{h}", np.concatenate([bias(r, r), bias(128 + r, np.arange(256)), b2], axis=1))
    masks = []
    for c in LEVELS[1:]:
        if c:
            m = (r[:, None] // (2 * c) == r[None, :] // (2 * c)) & (r[:, None] % (2 * c) < c) & (r[None, :] % (2 * c) >= c)
        else:
            m = r[:, None] == r[None, :]
        s = m & (r[:, None] >= 64) & (r[None, :] >= 64)
        masks.append(np.concatenate([m, s, m], axis=1))
    return np.concatenate(parts, axis=1), at, np.concatenate(masks, axis=1).astype(np.float32)


def build(nc, ins, outs, table_at):
    ctx = ExitStack()
    with ctx:
        def sb(name, shape, dt=F32):
            return ctx.enter_context(nc.sbuf_tensor(name, shape, dt))

        def sem(name):
            return ctx.enter_context(nc.semaphore(name))

        raw = [sb(f"raw{s}", [P, 16 * P]) for s in range(2)]
        w_h = [sb(f"w_h{s}", [P, 16 * P], F32R) for s in range(2)]
        w_l = [sb(f"w_l{s}", [P, 16 * P], F32R) for s in range(2)]
        x = sb("x", [P, KD, T])
        y = sb("y", [P, KD, T])
        NCONST = sum(n for _, n in table_at.values())
        FIRST = table_at["rot"][0]
        N_PAR = 16 * 12 * DEPTH
        const = sb("const", [P, NCONST])
        mask = sb("mask", [P, 8, 3 * P], U8)
        par = sb("par", [P, DEPTH, PARAMS])
        a2 = sb("a2", [RANK, DEPTH, P])
        lam_e = sb("lam_e", [P, DEPTH * 2])
        par_l = sb("par_l", [P, PARAMS])
        gain_l = par_l[:, 0:6 * KD].rearrange("p (a k) -> p a k", a=6)
        small_l = par_l[:, 6 * KD:PARAMS]
        a2_l = sb("a2_l", [RANK, P])
        rs = sb("rs", [P, T])
        var = sb("var", [P, 4])
        inv = sb("inv", [P, 4])
        ssum = sb("ssum", [P, T])
        ssum_x = sb("ssum_x", [P, T])
        sq_2 = sb("sq_2", [P, 2 * T])
        sq = [sq_2[:, 0:T], sq_2[:, T:2 * T]]
        gk_tok = sq_2[:, 0:3 * P].rearrange("p (i c) -> p i c", i=3)

        base = nc.sbuf_base

        def placer(start):
            here = [start]

            def place(name, shape, dt=F32):
                size = (1 if dt == U8 else 4) * int(np.prod(shape[1:]))
                t = nc.alloc_sbuf_tensor_at(name, shape, dt, offset=here[0])
                here[0] += (size + 31) // 32 * 32
                return t
            return place, here

        place, here = placer(base)
        xn_h = place("xn_h", [P, KD, T], F32R)
        xn_l = place("xn_l", [P, KD, T], F32R)
        region = here[0]
        place, here2 = placer(base)
        rv_tok = place("rv_tok", [P, 3, 256])
        rk_tok = place("rk_tok", [P, 3, 256])
        assert here2[0] <= region
        place, here = placer(region)
        hid_h = place("hid_h", [P, KF, T], F32R)
        hid_l = place("hid_l", [P, KF, T], F32R)
        gate = [place(f"gate{s}", [P, T]) for s in range(2)]
        up = [place(f"up{s}", [P, T]) for s in range(2)]
        assert here[0] <= nc.sbuf_usable_end
        place, here = placer(region)
        x_in = place("x_in", [P, 3, D])
        mask_in = place("mask_in", [P, 8 * 3 * P])
        par_in = place("par_in", [P, P])
        lam_in = place("lam_in", [P, DEPTH, 4, DK_D])
        lam_p = place("lam_p", [P, DEPTH * 2, DK_D])
        place, here = placer(region)
        z = place("z", [P, NZ, T])
        alr = place("alr", [P, T])
        dk_tok = place("dk_tok", [P, 3, H, P])
        dv_tok = place("dv_tok", [P, 3, H, P])
        gv_tok = place("gv_tok", [P, 3, 256])
        scores = place("scores", [P, H, 4, P])
        probs = place("probs", [P, 2, 2, 3 * P])
        probs_t = place("probs_t", [P, 3, P])
        kc_t = place("kc_t", [P, H, PAST])
        vc = place("vc", [P, 2, H * P])
        decay = place("decay", [P, T])
        wgt = place("wgt", [P, T])
        q_w = place("q_w", [P, T])
        k_w = place("k_w", [P, T])
        s0_a = place("s0_a", [P, DV_A])
        s0_r = place("s0_r", [P, 2, DV_R])
        q_s = place("q_s", [P, 2, T_S])
        st_a = place("st_a", [P, 2, DV_A])
        st_r = place("st_r", [P, 2, 2, DV_R])
        tiny = place("tiny", [P, 32])
        var_h = place("var_h", [P, 3, 12])
        inv_h = place("inv_h", [P, 3, 12])
        assert here[0] <= nc.sbuf_usable_end, (here[0], nc.sbuf_usable_end)
        kc_raw = scores[:, :, :, :].rearrange("p h b c -> p (h b c)")[:, 0:2 * H * P].rearrange("p (i c) -> p i c", i=2)

        ps_g = ctx.enter_context(nc.psum_tensor("ps_g", [P, 4, 512], F32))
        ps_m = ctx.enter_context(nc.psum_tensor("ps_m", [P, 4, 512], F32))

        def C(name):
            a, n = table_at[name]
            return const[:, a:a + n]

        x_loaded = sem("x_loaded")
        par_loaded = sem("parameters_loaded")
        tables_loaded = sem("tables_loaded")
        masks_loaded = sem("masks_loaded")
        masks_cast = sem("masks_cast")
        par_mm = sem("par_mm")
        raw_in = [sem(f"raw_in{s}") for s in range(2)]
        w_hi, w_lo, w_used = sem("w_hi"), sem("w_lo"), sem("w_used")
        evac = sem("evac")
        x_new = sem("x_new")
        y_norm = sem("y_norm")
        xn_hi, xn_lo = sem("xn_hi"), sem("xn_lo")
        sq_x = sem("sq_x")
        x_ss = sem("x_ss")
        x_add = sem("x_add")
        ss_mm = sem("ss_mm")
        ss_var = sem("ss_var")
        ss_sqrt = sem("ss_sqrt")
        inv_out = sem("inv_out")
        rs_mm = sem("rs_mm")
        up_mul, silu, prod = sem("gate_scaled"), sem("silu_done"), sem("hidden_product")
        hid_hi, hid_lo = sem("hid_hi"), sem("hid_lo")
        y_sq = sem("y_sq")
        y_acc = sem("y_acc")
        past_in = sem("past_in")
        kv_stored, st_stored = sem("keys_and_values_stored"), sem("states_stored")
        params = sem("params")
        y_stored = sem("y_stored")
        passed = sem("passed")
        y_mm, y_rows = sem("y_mm"), sem("y_rows")
        x_mm = sem("x_mm")
        mem_set = sem("scores_zeroed")
        lam_s = sem("lam_s")
        mix = {k: sem(f"mix_{k}") for k in ("pe", "act", "dve", "pool")}
        place_of = {k: {name: n + 1 for n, name in enumerate(v)} for k, v in MILESTONES.items()}
        reached = {"pe": 0, "act": 0, "dve": 0, "pool": 0}

        def mark(who, instruction, name):
            reached[who] += 1
            assert place_of[who][name] == reached[who], (who, name, MILESTONES[who][reached[who] - 1])
            instruction.then_inc(mix[who], 1)

        def after(e, l, who, name):
            e.wait_ge(mix[who], l * len(MILESTONES[who]) + place_of[who][name])

        def then_pass(e):
            e.sem_inc(passed, 1)

        block = ctx.enter_context(nc.Block())
        rearr = lambda t: t[:, :, :].rearrange("p a b -> p (a b)")

        @block.sync
        def _(sp):
            def load(l, u, s, src, k, c):
                sp.wait_ge(w_lo, l * UNITS + u + 1)
                dst = raw[s][:, 0:k * c].rearrange("p (k c) -> p k c", k=k)
                sp.dma_start(dst, src).then_inc(raw_in[s], 16)

            def rows(w, l, r0, nk, c0, nc_):
                return w[bass.ds(l, 1), r0:r0 + nk * P, c0].rearrange("a (k p) c -> p (a k) c", p=P)

            def ffn(l, u0, w_up, w_down):
                with sp.Fori(0, N_UP // 2) as j:
                    for s in range(2):
                        sp.wait_ge(w_lo, l * UNITS + (2 * j + (u0 + s + 1)))
                        dst = raw[s][:, :].rearrange("p (g k c) -> p g k c", g=2, k=KD)
                        for g in range(2):
                            src = w_up[bass.ds(l, 1), :, bass.ds(2 * P * j + (g * D_FF + s * P), P)]
                            ins_ = sp.dma_start(dst[:, g], src.rearrange("a (k p) c -> p (a k) c", p=P))
                            ins_.then_inc(raw_in[s], 16)
                with sp.Fori(0, KD) as m:
                    for s in range(2):
                        src = w_down[bass.ds(l, 1), s * HALF_DOWN * P:(s + 1) * HALF_DOWN * P, bass.ds(P * m, P)]
                        load(l, 2 * m + (u0 + N_UP + s), s, src.rearrange("a (k p) c -> p (a k) c", p=P), HALF_DOWN, P)

            def pairs(l, u0, n, w, c0):
                with sp.Fori(0, n // 2) as j:
                    for s in range(2):
                        src = w[bass.ds(l, 1), :, bass.ds(4 * P * j + (c0 + 2 * s * P), 2 * P)]
                        load(l, 2 * j + (u0 + s), s, src.rearrange("a (k p) c -> p (a k) c", p=P), KD, 2 * P)

            with sp.Fori(0, DEPTH) as l:
                ffn(l, U_F1, ins["ffn1_w_up"], ins["ffn1_w_down"])
                w = ins["w_in"]
                load(l, U_MIX, 0, w[bass.ds(l, 1), :, 0:P].rearrange("a (k p) c -> p (a k) c", p=P), KD, P)
                for v in range(1, N_MIX):
                    c = RANK + UNIT_TILE[v] * P
                    load(l, U_MIX + v, v % 2, w[bass.ds(l, 1), :, c:c + 2 * P].rearrange("a (k p) c -> p (a k) c", p=P), KD, 2 * P)
                pairs(l, U_OUT, N_OUT, ins["w_out"], 0)
                ffn(l, U_F2, ins["ffn2_w_up"], ins["ffn2_w_down"])

        def raw_after(u):
            tot = 0
            for v in range(u % 2, u + 1, 2):
                up_unit = v < N_UP or U_F2 <= v < U_F2 + N_UP
                tot += 32 if up_unit else 16
            return tot
        RAW_LAYER = raw_after(UNITS - 1)
        assert raw_after(UNITS - 2) == RAW_LAYER

        @block.gpsimd
        def _(pool):
            def sum_x(l, n):
                for k in range(1, KD):
                    pool.wait_ge(sq_x, l * 3 * KD + (n * KD + k + 1))
                    if k > 1:
                        pool.wait_ge(x_add, l * 3 * (KD - 1) + (n * (KD - 1) + k - 1))
                    a = y[:, 0, :] if k == 1 else ssum_x[:, :]
                    pool.tensor_tensor(ssum_x[:, :], a, y[:, k, :], ALU.add).then_inc(x_add, 1)
                pool.wait_ge(x_add, (l * 3 + n + 1) * (KD - 1))
                pool.sem_inc(x_ss, 1)

            def add_y(l, m):
                for k in range(KD):
                    pool.wait_ge(y_norm, l * 3 * KD + (m * KD + k + 1))
                    pool.tensor_tensor(x[:, k, :], x[:, k, :], y[:, k, :], ALU.add).then_inc(x_new, 1)

            pool.dma_start(mask_in[:, :], ins["masks"]).then_inc(masks_loaded, 16)
            pool.wait_ge(masks_loaded, 16)
            pool.tensor_copy(mask[:, :, :].rearrange("p a b -> p (a b)"), mask_in[:, :]).then_inc(masks_cast, 1)

            def dist(l, n):
                c = LEVELS[n]
                cols = slice(0, T_P if c >= 64 else T)
                if n:
                    after(pool, l, "pool", f"qk{n - 1}")
                else:
                    after(pool, l, "dve", "decay")
                v = decay[:, cols].rearrange("p (b c) -> p b c", c=2 * c)
                mark("pool", pool.tensor_tensor(wgt[:, cols].rearrange("p (b c) -> p b c", c=2 * c), v,
                                                v[:, :, c - 1:c].broadcast_to([P, v.shape[1], 2 * c]), ALU.subtract), f"dist{n}")

            def qk(l, n):
                cols = slice(0, T_P if LEVELS[n] >= 64 else T)
                after(pool, l, "act", f"weight{n}")
                if n:
                    after(pool, l, "pe", f"level{n - 1}")
                pool.tensor_tensor(q_w[:, cols], z[:, GQ, cols], wgt[:, cols], ALU.mult)
                mark("pool", pool.tensor_tensor(k_w[:, cols], z[:, GK, cols], wgt[:, cols], ALU.mult), f"qk{n}")

            with pool.Fori(0, DEPTH) as l:
                sum_x(l, 0)
                pool.wait_ge(w_used, l * UNITS + (U_MIX + 2))
                then_pass(pool)
                pool.dma_start(kc_raw, ins["cache_diff_k"][bass.ds(l, 1), 0].rearrange("a (i p) h d -> p (a i) (h d)", p=P)
                               ).then_inc(past_in, 16)
                pool.dma_start(vc[:, :, :], ins["cache_diff_v"][bass.ds(l, 1), 0].rearrange("a (i p) h d -> p (a i) (h d)", p=P)
                               ).then_inc(past_in, 16)
                pool.dma_start(s0_a[:, :], ins["state_gla"][bass.ds(l, 1), 0].rearrange("a h d v -> (a h d) v")
                               ).then_inc(past_in, 16)
                pool.dma_start(s0_r[:, :, :], ins["state_ret"][bass.ds(l, 1), 0].rearrange("a (j h) d v -> (a h d) j v", j=2)
                               ).then_inc(past_in, 16)
                add_y(l, 0)
                sum_x(l, 1)
                for kind, *arg in SCHEDULE:
                    n = arg[0] if arg else None
                    if kind == "logit":
                        dist(l, 0)
                    elif kind == "past":
                        after(pool, l, "pe", "kct1")
                        then_pass(pool)
                        pool.memset(scores[:, :, :, :], 0.0).then_inc(mem_set, 1)
                    elif kind == "level":
                        if n == 0:
                            qk(l, 0)
                        if n < 7:
                            dist(l, n + 1)
                            qk(l, n + 1)
                    elif kind == "gla_out":
                        after(pool, l, "dve", "gla_state")
                        then_pass(pool)
                        for i, name in enumerate(("prompt", "sample")):
                            pool.dma_start(outs[f"state_gla_{name}"][bass.ds(l, 1), 0].rearrange("a h d v -> (a h d) v"),
                                           st_a[:, i, :]).then_inc(st_stored, 16)
                    elif kind == "tok" and n == 3:
                        after(pool, l, "act", "tok3")
                        then_pass(pool)
                        for t, name in ((dk_tok, "k"), (dv_tok, "v")):
                            o = outs[f"new_{name}_prompt"]
                            pool.dma_start(o[bass.ds(l, 1), 0].rearrange("a (i p) h d -> p (a i) (h d)", p=P),
                                           t[:, 0:2, :, :].rearrange("p i h d -> p i (h d)")).then_inc(kv_stored, 16)
                            o = outs[f"new_{name}_sample"]
                            pool.dma_start(o[bass.ds(l, 1), 0].rearrange("a p h d -> p (a h d)"),
                                           t[64:128, 2, :, :].rearrange("p h d -> p (h d)")).then_inc(kv_stored, 16)
                    elif kind == "ret_out":
                        after(pool, l, "dve", "ret_state")
                        then_pass(pool)
                        for i, name in enumerate(("prompt", "sample")):
                            pool.dma_start(outs[f"state_ret_{name}"][bass.ds(l, 1), 0].rearrange("a (j h) d v -> (a h d) j v", j=2),
                                           st_r[:, i, :, :]).then_inc(st_stored, 16)
                add_y(l, 1)
                sum_x(l, 2)
                add_y(l, 2)
            pool.wait_ge(kv_stored, DEPTH * 4 * 16)
            pool.wait_ge(st_stored, DEPTH * 4 * 16)

        @block.tensor
        def _(pe):
            pe.sem_inc(w_used, 2)

            def product(out, s, blk, xh, xl, first, last):
                w = slice(blk * P, blk * P + P)
                pe.matmul(out, w_h[s][:, w], xl, start=first, stop=False)
                pe.matmul(out, w_l[s][:, w], xh, start=False, stop=False)
                return pe.matmul(out, w_h[s][:, w], xh, start=False, stop=last)

            def part(l, u, g, s, k0, k1, ready=None, tiles=2, k_major=False, order=None):
                if k0 == 0:
                    pe.wait_ge(w_lo, l * UNITS + u + 3)
                    pe.wait_ge(evac, l * GROUPS + g + 1)
                for i in range(k0, k1):
                    k = order[i] if order else i
                    if ready is not None:
                        ready(i)
                    for n in range(tiles):
                        blk = k * tiles + n if k_major else n * KD + k
                        mm = product(ps_g[:, 2 * s + n, 0:T], s, blk, xn_h[:, k, :], xn_l[:, k, :], i == 0, i == KD - 1)
                if k1 == KD:
                    mm.then_inc(w_used, 1)

            def first_two(l, u, g, n, tiles=2, k_major=False, order=None, between=None):
                ready = lambda i: pe.wait_ge(xn_lo, l * 32 + (8 * n + i + 1))
                for i in range(4):
                    part(l, u, g, 0, i, i + 1, ready, tiles, k_major, order)
                    part(l, u + 1, g + 1, 1, i, i + 1, None, 2, k_major, order)
                part(l, u, g, 0, 4, 8, ready, tiles, k_major, order)
                if between:
                    between()
                part(l, u + 1, g + 1, 1, 4, 8, None, 2, k_major, order)

            def stat_x(l, n, m):
                pe.wait_ge(x_ss, l * 3 + m + 1)
                for i in range(3):
                    mm = pe.matmul(ps_m[:, 0, i:i + 1], ssum_x[:, TOK[i]:TOK[i] + P], C("ones")[:, 0:1], start=i == 0, stop=True,
                                   skip_group_check=True)
                mm.then_inc(ss_mm, 1)

            def stat_y(l, n, m):
                pe.wait_ge(y_acc, (l * 3 + m + 1) * (KD - 1) + 2)
                for i in range(3):
                    pe.matmul(ps_m[:, 0, i:i + 1], ssum[:, TOK[i]:TOK[i] + P], C("ones")[:, 0:1], start=i == 0, stop=False,
                              skip_group_check=True)
                pe.wait_ge(y_sq, (l * 3 + m + 1) * KD)
                for i in range(3):
                    mm = pe.matmul(ps_m[:, 0, i:i + 1], sq[1][:, TOK[i]:TOK[i] + P], C("ones")[:, 0:1], start=False, stop=True,
                                   skip_group_check=True)
                mm.then_inc(ss_mm, 1)

            def spread(l, n):
                pe.wait_ge(inv_out, l * 6 + n + 1)
                for i in range(3):
                    mm = pe.matmul(ps_m[:, 1, TOK[i]:TOK[i] + P], inv[:, i:i + 1].broadcast_to([P, P]), C("ident"),
                                   start=True, stop=True)
                mm.then_inc(rs_mm, 1)

            def ffn(l, u0, g0, norm, n, m):
                first_two(l, u0, g0, n, between=lambda: stat_x(l, norm, m))
                spread(l, norm)
                with pe.Fori(1, N_UP // 2) as j:
                    for s in range(2):
                        part(l, 2 * j + (u0 + s), 2 * j + (g0 + s), s, 0, KD)
                with pe.Fori(0, KD // 2) as m_:
                    for b in range(2):
                        for s in range(2):
                            pe.wait_ge(w_lo, l * UNITS + (4 * m_ + (u0 + N_UP + 2 * b + s + 3)))
                            if s == 0:
                                pe.wait_ge(evac, l * GROUPS + (2 * m_ + (g0 + N_UP + b + 1)))
                                pe.wait_ge(hid_lo, l * 2 * KF + (KF * (norm // 4) + HALF_DOWN))
                            else:
                                pe.wait_ge(hid_lo, l * 2 * KF + (KF * (norm // 4) + KF))
                            for i in range(HALF_DOWN):
                                k = s * HALF_DOWN + i
                                mm = product(ps_g[:, 2 * b, 0:T], s, i, hid_h[:, k, :], hid_l[:, k, :], k == 0, k == KF - 1)
                            mm.then_inc(w_used, 1)
                stat_y(l, norm + 1, norm // 2)
                spread(l, norm + 1)

            pe.wait_ge(x_loaded, 4 * 16)
            for k in range(KD):
                if k >= 2:
                    pe.wait_ge(x_new, k - 1)
                for i in range(3):
                    mm = pe.transpose(ps_m[:, k % 2, TOK[i]:TOK[i] + P], x_in[:, i, k * P:(k + 1) * P], C("ident"))
                mm.then_inc(x_mm, 1)
                if k == 1:
                    pe.wait_ge(par_loaded, N_PAR)
                    pe.transpose(ps_m[:, 2, 0:DEPTH * ROWS], par_in[0:DEPTH * ROWS, :], C("ident")[0:DEPTH * ROWS, 0:DEPTH * ROWS]
                                 ).then_inc(par_mm, 1)

            def heads_out(bank0, v_tok, s0, q0):
                for h in range(H):
                    out = ps_m[64 * (h % 2):64 * (h % 2) + 64, bank0 + h // 2, :]
                    v = lambda i: v_tok[:, i, h * 64:(h + 1) * 64]
                    sc = scores[:, h, :, :].rearrange("p b c -> p (b c)")
                    pe.matmul(out[:, 0:256], v(0), sc[:, 256:512], start=True, stop=False, skip_group_check=True)
                    pe.matmul(out[:, 128:256], v(1), sc[:, 0:128], start=False, stop=False, skip_group_check=True)
                    pe.matmul(out[:, 256:320], v(2), sc[:, 192:256], start=False, stop=False, skip_group_check=True)
                    mm = pe.matmul(out[:, 256:320], s0(h), q0(h), start=False, stop=True, skip_group_check=True)
                return mm

            def tok(l, n, bank):
                pe.wait_ge(evac, l * GROUPS + (G_MIX + UNIT_TILE.index(SPLITS[n][0] // 2 * 2) + 3))
                for i in range(3):
                    mm = pe.transpose(bank[:, i * P:(i + 1) * P], z[:, SPLITS[n][0], TOK[i]:TOK[i] + P], C("ident"))
                mark("pe", mm, f"tok{n}")

            def m2_free(l, n):
                if n >= 3:
                    after(pe, l, "act", f"att_t{n - 3}")
                if 5 <= n < 9:
                    after(pe, l, "dve", f"rot{n - 5}")
                if 9 <= n < 13:
                    after(pe, l, "dve", f"ret_s{n - 9}")

            def mixer_step(l, kind, n):
                if kind == "past":
                    pe.wait_ge(past_in, (l + 1) * 64)
                    after(pe, l, "dve", "minus")
                    for i in range(2):
                        for h in range(H):
                            mm = pe.transpose(ps_m[:, i, h * P:(h + 1) * P], kc_raw[:, i, h * P:(h + 1) * P], C("ident"))
                        mark("pe", mm, f"kct{i}")
                elif kind == "logit":
                    pe.wait_ge(evac, l * GROUPS + (G_MIX + 3))
                    mark("pe", pe.matmul(ps_m[:, 0, 0:T], a2_l[:, :], alr[0:RANK, :], start=True, stop=True), "logit")
                elif kind == "tok":
                    if n in (4, 5):
                        after(pe, l, "dve", "gla_o")
                    elif n not in (8, 9):
                        after(pe, l, "act", {6: "tok4", 7: "tok5", 0: "tok6", 1: "tok7", 2: "tok0", 3: "tok1"}[n])
                    tok(l, n, ps_m[:, 2 + n % 2, :])
                elif kind == "level":
                    if n < 8:
                        after(pe, l, "pool", f"qk{n}")
                    if n:
                        after(pe, l, "dve", f"score{n - 1}")
                    else:
                        after(pe, l, "act", "kct1")
                        after(pe, l, "act", "tok9")
                    for h in range(H):
                        r = slice(h * 32, h * 32 + 32)
                        todo = [(3, 0, 1)] if n == 0 else [(0, 1, 1), (2, 0, 0)] if n == 1 else [(0, 1, 1), (1, 2, 2), (2, 0, 0)]
                        for at, si, ti in todo:
                            qs, ks = (z[:, GQ, :], z[:, GK, :]) if n == 8 else (q_w[:, :], k_w[:, :])
                            mm = pe.matmul(ps_m[:, h, at * P:(at + 1) * P], ks[r, TOK[si]:TOK[si] + P],
                                           qs[r, TOK[ti]:TOK[ti] + P], start=True, stop=True)
                    mark("pe", mm, f"level{n}")
                elif kind == "gla_keys":
                    after(pe, l, "dve", "k_end")
                    for i in range(3):
                        mm = pe.transpose(ps_m[:, 2, i * P:(i + 1) * P], k_w[:, TOK[i]:TOK[i] + P], C("ident"))
                    mark("pe", mm, "ketok")
                elif kind == "gla_out":
                    after(pe, l, "act", "ketok")
                    for i in range(2):
                        pe.matmul(ps_m[:, 0, 0:256], gk_tok[:, i, :], gv_tok[:, i, :], start=i == 0, stop=i == 1)
                    mark("pe", pe.matmul(ps_m[:, 1, 0:256], gk_tok[64:128, 2, :], gv_tok[64:128, 2, :], start=True, stop=True),
                         "gla_state")
                    mark("pe", heads_out(2, gv_tok, lambda h: s0_a[h * 32:h * 32 + 32, :], lambda h: q_s[h * 32:h * 32 + 32, 0, :]),
                         "gla_o")
                elif kind == "att":
                    if n >= 2:
                        h, b = ATT[n - 2]
                        m2_free(l, n)
                        if n == 2:
                            after(pe, l, "act", "tok2")
                        after(pe, l, "dve", f"att_a{n - 2}")
                        for kt in range(KEYS[b]):
                            mm = pe.transpose(ps_m[:, 2, kt * P:(kt + 1) * P], probs[:, n % 2, 0, kt * P:(kt + 1) * P], C("ident"))
                        mark("pe", mm, f"att_t{n - 2}")
                    if n < 12:
                        h, b = ATT[n]
                        if n:
                            after(pe, l, "dve", f"att_max{n - 1}")
                        else:
                            after(pe, l, "dve", "gla_state")
                        keys = KEYS[b] * P
                        for m in range(2):
                            r = slice(64 * m, 64 * m + 64)
                            q = z[r, DQ + h, TOK[b]:TOK[b] + P]
                            if b < 2:
                                mm = pe.matmul(ps_m[:, m, 0:keys], q, z[r, DKK + h, 0:keys], start=True, stop=True)
                            else:
                                pe.matmul(ps_m[:, m, 0:PAST], q, kc_t[r, h, :], start=True, stop=False, skip_group_check=True)
                                mm = pe.matmul(ps_m[:, m, PAST:keys], q, z[r, DKK + h, TOK[2]:TOK[2] + P], start=False, stop=True,
                                               skip_group_check=True)
                        mark("pe", mm, f"att_s{n}")
                    if n >= 2:
                        h, b = ATT[n - 2]
                        after(pe, l, "act", f"att_t{n - 2}")
                        if b == 0 and h:
                            after(pe, l, "act", f"att_o{n - 3}")
                        if n == 2:
                            after(pe, l, "act", "tok3")
                        for kt in range(KEYS[b]):
                            v = vc[:, kt, h * P:(h + 1) * P] if b == 2 and kt < 2 else dv_tok[:, kt, h, :]
                            o, a = (ps_m[:, 3, b * P:(b + 1) * P], probs_t[:, kt, :]) if b < 2 else \
                                   (ps_m[:, 3, 256:320], probs_t[:, kt, 64:128])
                            mm = pe.matmul(o, v, a, start=b == 0 and kt == 0, stop=kt == KEYS[b] - 1, skip_group_check=True)
                        mark("pe", mm, f"att_o{n - 2}")
                elif kind == "rot":
                    after(pe, l, "act", f"att_t{n + 2}")
                    mark("pe", pe.matmul(ps_m[:, 2, 0:T], C("rot"), z[:, RQ + n, :], start=True, stop=True), f"rot{n}")
                elif kind == "ret_s":
                    after(pe, l, "act", f"att_t{n + 6}")
                    after(pe, l, "dve", "rot3")
                    r = slice(64 * (n % 2), 64 * (n % 2) + 64)
                    q, k = z[r, RQ + n // 2, :], z[r, RK + n // 2, :]
                    bank = ps_m[:, 2, :]
                    pe.matmul(bank[:, 256:512], k[:, 0:P], q[:, 0:256], start=True, stop=False, skip_group_check=True)
                    pe.matmul(bank[:, 0:128], k[:, P:2 * P], q[:, P:2 * P], start=False, stop=False, skip_group_check=True)
                    mm = pe.matmul(bank[:, 128:256], k[:, TOK[2]:T], q[:, TOK[2]:T], start=False, stop=True, skip_group_check=True)
                    mark("pe", mm, f"ret_s{n}")
                elif kind == "ret_keys":
                    pe.wait_ge(evac, l * GROUPS + (G_MIX + N_MIX + 2))
                    for i in range(2):
                        tok(l, 10 + i, ps_g[:, 2 + i, :])
                    after(pe, l, "dve", "ret_k")
                    for j in range(2):
                        for i in range(3):
                            mm = pe.transpose(ps_g[:, j, i * P:(i + 1) * P], (k_w, wgt)[j][:, TOK[i]:TOK[i] + P], C("ident"))
                        mark("pe", mm, f"ret_kt{j}")
                elif kind == "ret_out":
                    after(pe, l, "act", "ret_kt1")
                    after(pe, l, "dve", "att_max11")
                    for j in range(2):
                        c = slice(j * P, (j + 1) * P)
                        for i in range(2):
                            pe.matmul(ps_g[:, j, 0:P], rk_tok[:, i, c], rv_tok[:, i, c], start=i == 0, stop=i == 1)
                        mm = pe.matmul(ps_g[:, j, P:2 * P], rk_tok[64:128, 2, c], rv_tok[64:128, 2, c], start=True, stop=True,
                                       skip_group_check=True)
                    mark("pe", mm, "ret_state")
                    half = lambda h: slice(64 * (h % 2), 64 * (h % 2) + 64)
                    mark("pe", heads_out(0, rv_tok, lambda h: s0_r[half(h), h // 2, :], lambda h: q_s[half(h), h // 2, :]), "ret_o")
                    after(pe, l, "dve", "ret_o")
                    for j in range(2):
                        mm = pe.matmul(ps_g[:, 2 + j, 0:T], C("mean64"), y[:, 6 + j, :], start=True, stop=True)
                    mark("pe", mm, "ret_mu")
                elif kind == "norms":
                    after(pe, l, "dve", "ret_state")
                    after(pe, l, "act", "squares")
                    for q in HEAD_ORDER:
                        c, w, ind = HEAD_AT[q]
                        for i in range(3):
                            mm = pe.matmul(ps_g[:, 0, 12 * i + c:12 * i + c + w], z[:, DQ + q, TOK[i]:TOK[i] + P], C(ind),
                                           start=q == 0 and i == 0, stop=True, skip_group_check=True)
                    mark("pe", mm, "ms")
                    after(pe, l, "dve", "inv")
                    for j, q in enumerate(HEAD_ORDER):
                        c, w, _ = HEAD_AT[q]
                        if j >= 2:
                            after(pe, l, "dve", f"head{HEAD_ORDER[j - 2]}")
                        for i in range(3):
                            for h in range(w):
                                n = P // w
                                mm = pe.matmul(ps_m[h * n:h * n + n, 1 + j % 2, TOK[i]:TOK[i] + P],
                                               inv_h[:, i, c + h:c + h + 1].broadcast_to([P, n]), C("ident"), start=True, stop=True)
                        mark("pe", mm, f"spread{q}")

            with pe.Fori(0, DEPTH) as l:
                ffn(l, U_F1, G_F1, 0, 0, 0)
                first_two(l, U_MIX, G_MIX, 1, tiles=1, k_major=True, between=lambda: stat_x(l, 2, 1))
                spread(l, 2)
                pe.wait_ge(tables_loaded, 16)
                for kind, *arg in SCHEDULE:
                    if kind == "part":
                        v, k0, k1 = arg
                        part(l, U_MIX + v, G_MIX + v, v % 2, k0, k1, k_major=True)
                    else:
                        mixer_step(l, kind, arg[0] if arg else None)
                first_two(l, U_OUT, G_OUT, 2, k_major=True, order=HEAD_ORDER)
                for s in range(2):
                    part(l, U_OUT + 2 + s, G_OUT + 2 + s, s, 0, KD, k_major=True)
                stat_y(l, 3, 1)
                spread(l, 3)
                ffn(l, U_F2, G_F2, 4, 3, 2)

            pe.wait_ge(x_new, (3 * DEPTH + 1) * KD)
            for n in range(3 * 2):
                if n >= 2:
                    pe.wait_ge(y_rows, n - 1)
                for q in range(4):
                    k = 4 * (n % 2) + q
                    i = n // 2
                    mm = pe.transpose(ps_m[:, n % 2, q * P:(q + 1) * P], x[:, k, TOK[i]:TOK[i] + P], C("ident"))
                mm.then_inc(y_mm, 1)

        def hi_of_unit(act, l, u, s, landed, cols):
            act.wait_ge(raw_in[s], l * RAW_LAYER + landed)
            act.wait_ge(w_used, l * UNITS + u + 1)
            act.activation(w_h[s][:, 0:cols], raw[s][:, 0:cols], ACT.Copy).then_inc(w_hi, 1)

        def lo_of_unit(dve, l, u, s, cols):
            dve.wait_ge(w_hi, l * UNITS + u + 1)
            dve.tensor_tensor(w_l[s][:, 0:cols], raw[s][:, 0:cols], w_h[s][:, 0:cols], ALU.subtract).then_inc(w_lo, 1)

        def unit_cols(u):
            down = N_UP <= u < U_MIX or u >= U_F2 + N_UP
            return HALF_DOWN * P if down else KD * P if u == U_MIX else 2 * KD * P

        def hi(act, l, u):
            hi_of_unit(act, l, u, u % 2, raw_after(u), unit_cols(u))

        def lo(dve, l, u):
            lo_of_unit(dve, l, u, u % 2, unit_cols(u))

        @block.scalar
        def _(act):
            act.dma_start(x_in[:, 0:2, :], ins["x_prompt"][0].rearrange("(i p) c -> p i c", p=P)).then_inc(x_loaded, 16)
            act.dma_start(x_in[0:64, 2, :], ins["x_prompt"][0, TOK[2]:T_P, :]).then_inc(x_loaded, 16)
            act.dma_start(x_in[64:128, 2, :], ins["x_sample"][0]).then_inc(x_loaded, 16)
            act.dma_start(const[:, 0:FIRST], ins["tables"][:, 0:FIRST]).then_inc(x_loaded, 16)
            norms = ("ffn1_norm_pre", "ffn1_norm_post", "mix_norm_pre", "mix_norm_post", "ffn2_norm_pre", "ffn2_norm_post")
            for l in range(DEPTH):
                for n, name in enumerate(norms):
                    r = l * ROWS + n * KD
                    act.dma_start(par_in[r:r + KD, :], ins[name][l].rearrange("(k p) -> k p", p=P)).then_inc(par_loaded, 16)
                r = l * ROWS + 6 * KD
                act.dma_start(par_in[r + C_BIAS:r + C_BIAS + 1, :], ins["b_gla_a"][l:l + 1, :]).then_inc(par_loaded, 16)
                act.dma_start(par_in[r + C_GLA:r + C_GLA + 2, :], ins["gla_norm"][l].rearrange("(j h) v -> j (h v)", j=2)
                              ).then_inc(par_loaded, 16)
                act.dma_start(par_in[r + C_ATT:r + C_ATT + 1, :], ins["diff_subln"][l:l + 1, :]).then_inc(par_loaded, 16)
                act.dma_start(par_in[r + C_RET:r + C_RET + 2, :], ins["ret_norm"][l].rearrange("(j h) v -> j (h v)", j=2)
                              ).then_inc(par_loaded, 16)
                act.dma_start(a2[:, l, :], ins["w_gla_a2"][l]).then_inc(par_loaded, 16)
                act.dma_start(lam_in[:, l, :, :].rearrange("p a b -> p (a b)"),
                              ins["diff_lambda"][l:l + 1, :, :].rearrange("o a b -> o (a b)").broadcast_to([P, 4 * DK_D])
                              ).then_inc(par_loaded, 16)
            act.dma_start(const[:, FIRST:], ins["tables"][:, FIRST:]).then_inc(tables_loaded, 16)
            act.wait_ge(lam_s, 1)
            act.activation(lam_e[:, :], lam_e[:, :], ACT.Exp).then_inc(lam_s, 1)

            def tile(t, k):
                return t[:, k, :] if isinstance(k, int) else t[:, bass.ds(k, 1), :].rearrange("p a t -> p (a t)")

            def split_hi(l, n, k, src, gain):
                scale = 1.0 if gain is None else gain_l[:, gain, k:k + 1]
                act.activation(xn_h[:, k, :], src[:, k, :], ACT.Copy, scale=scale).then_inc(xn_hi, 1)

            def root(l, n):
                act.wait_ge(ss_var, l * 6 + n + 1)
                act.activation(var[:, 0:3], var[:, 0:3], ACT.Sqrt).then_inc(ss_sqrt, 1)

            def pre(l, n, norm, m):
                for k in range(KD):
                    act.wait_ge(x_new, l * 3 * KD + (m * KD + k + 1))
                    split_hi(l, n, k, x, norm)
                for k in range(KD):
                    act.activation(y[:, k, :], x[:, k, :], ACT.Square).then_inc(sq_x, 1)
                act.preload_act_table(ACT.Sqrt)
                root(l, norm)

            def y_tile(l, m, phase, bank, b, gain, used, last):
                if used is not None:
                    act.wait_ge(w_used, used)
                act.wait_ge(y_acc, l * 3 * (KD - 1) + (m + (phase * (KD - 1) + 1)))
                act.activation(sq[b][:, :], ps_g[:, bank, 0:T], ACT.Square).then_inc(y_sq, 1)
                scale = gain_l[:, gain, m:m + 1] if isinstance(m, int) else gain_l[:, gain, bass.ds(m, 1)]
                i = act.activation(tile(y, m), ps_g[:, bank, 0:T], ACT.Copy, scale=scale)
                if last:
                    i.then_inc(evac, 1)

            def ffn(l, u0, norm, n, following):
                f, phase = norm // 4, norm // 2
                pre(l, n, norm, phase)
                act.preload_act_table(ACT.Silu)

                def up_step(v, s, landed, cols):
                    hi_of_unit(act, l, v + (u0 + 2), s, landed, cols)
                    act.wait_ge(up_mul, l * 2 * KF + (v + (KF * f + 1)))
                    act.activation(gate[s][:, :], gate[s][:, :], ACT.Silu).then_inc(silu, 1)
                    act.wait_ge(prod, l * 2 * KF + (v + (KF * f + 1)))
                    act.activation(tile(hid_h, v), up[s][:, :], ACT.Copy).then_inc(hid_hi, 1)

                with act.Fori(0, N_UP // 2 - 1) as j:
                    for s in range(2):
                        up_step(2 * j + s, s, 32 * j + raw_after(u0 + 2 + s), 2 * KD * P)
                for s in range(2):
                    up_step(N_UP - 2 + s, s, raw_after(u0 + N_UP + s), HALF_DOWN * P)
                d0 = u0 + N_UP

                def down_tile(m, b):
                    used = l * UNITS + (2 * m + (d0 + 4))
                    if isinstance(m, int) and m == KD - 1:
                        if following is not None:
                            hi(act, l, following)
                        act.preload_act_table(ACT.Sqrt)
                        y_tile(l, m, phase, 2 * b, b, norm + 1, used, True)
                        root(l, norm + 1)
                        if following is not None:
                            hi(act, l, following + 1)
                        return
                    hi_of_unit(act, l, 2 * m + (d0 + 2), 0, 16 * m + raw_after(d0 + 2), HALF_DOWN * P)
                    y_tile(l, m, phase, 2 * b, b, norm + 1, used, True)
                    hi_of_unit(act, l, 2 * m + (d0 + 3), 1, 16 * m + raw_after(d0 + 3), HALF_DOWN * P)

                with act.Fori(0, KD // 2 - 1) as j:
                    for b in range(2):
                        down_tile(2 * j + b, b)
                down_tile(KD - 2, 0)
                down_tile(KD - 1, 1)

            def tok(l, n, src):
                at = SPLITS[n][1]
                dst = dk_tok[:, :, at, :] if n < 4 else dv_tok[:, :, at, :] if n < 8 else \
                    (gv_tok if n < 10 else rv_tok)[:, :, at * P:(at + 1) * P]
                after(act, l, "pe", f"tok{n}")
                mark("act", act.activation(dst, src[:, 0:3 * P].rearrange("p (i c) -> p i c", i=3), ACT.Copy), f"tok{n}")

            def mixer_step(l, kind, n):
                if kind == "past":
                    for i in range(2):
                        after(act, l, "pe", f"kct{i}")
                        mark("act", act.activation(kc_t[:, :, i * P:(i + 1) * P], ps_m[:, i, :].rearrange("p (h c) -> p h c", h=H),
                                                   ACT.Copy), f"kct{i}")
                elif kind == "tok":
                    tok(l, n, ps_m[:, 2 + n % 2, :])
                elif kind == "logit":
                    after(act, l, "pe", "logit")
                    mark("act", act.activation(wgt[:, :], ps_m[:, 0, 0:T], ACT.Abs, bias=small_l[:, C_BIAS:C_BIAS + 1]), "abs")
                    act.drain()
                    act.activation(wgt[:, :], wgt[:, :], ACT.Exp, scale=-1.0)
                    act.drain()
                    mark("act", act.activation(wgt[:, :], wgt[:, :], ACT.Ln, bias=1.0), "softplus")
                elif kind == "level":
                    for v in ((0, 1) if n == 0 else (n + 1,) if n < 7 else ()):
                        cols = slice(0, T_P if LEVELS[v] >= 64 else T)
                        after(act, l, "pool", f"dist{v}")
                        act.activation(wgt[:, cols], wgt[:, cols], ACT.Abs)
                        act.drain()
                        mark("act", act.activation(wgt[:, cols], wgt[:, cols], ACT.Exp, scale=-1.0 / 16), f"weight{v}")
                elif kind == "gla_keys":
                    mark("act", act.activation(q_s[:, 0, :], decay[:, T_P:T], ACT.Exp, scale=1.0 / 16), "from_start")
                    for i, t in enumerate((T_P - 1, T - 1)):
                        act.activation(tiny[:, i:i + 1], decay[:, t:t + 1], ACT.Copy, scale=1.0 / 16)
                        act.activation(tiny[:, 2 + i:3 + i], decay[:, t:t + 1], ACT.Exp, scale=1.0 / 16)
                    act.drain()
                    after(act, l, "pool", "qk7")
                    act.activation(wgt[:, 0:T_P], decay[:, 0:T_P], ACT.Exp, scale=-1.0 / 16, bias=tiny[:, 0:1])
                    mark("act", act.activation(wgt[:, T_P:T], decay[:, T_P:T], ACT.Exp, scale=-1.0 / 16, bias=tiny[:, 1:2]), "to_end")
                    after(act, l, "pe", "ketok")
                    mark("act", act.activation(gk_tok[:, :, :], ps_m[:, 2, 0:3 * P].rearrange("p (i c) -> p i c", i=3), ACT.Copy),
                         "ketok")
                elif kind == "att":
                    if n >= 2:
                        i, keys = n - 2, KEYS[ATT[n - 2][1]]
                        after(act, l, "pe", f"att_t{i}")
                        mark("act", act.activation(probs_t[:, 0:keys, :], ps_m[:, 2, 0:keys * P].rearrange("p (k c) -> p k c", c=P),
                                                   ACT.Copy), f"att_t{i}")
                    if n < 12:
                        keys, s = KEYS[ATT[n][1]] * P, n % 2
                        after(act, l, "dve", f"att_max{n}")
                        for m in range(2):
                            p = probs[:, s, m, 0:keys]
                            e = act.activation(p, p, ACT.Exp, bias=tiny[:, 8 + 2 * s + m:9 + 2 * s + m],
                                               accum_out=tiny[:, 12 + 2 * s + m:13 + 2 * s + m])
                        mark("act", e, f"att_e{n}")
                    if n % 3 == 1 and n > 1:
                        after(act, l, "pe", f"att_o{n - 2}")
                        mark("act", act.activation(y[:, 2 + n // 3 - 1, :], ps_m[:, 3, 0:T], ACT.Copy), f"att_o{n - 2}")
                elif kind == "ret_keys":
                    act.wait_ge(evac, l * GROUPS + (G_MIX + N_MIX + 2))
                    act.activation(z[:, GR:GR + 2, :], z[:, GR:GR + 2, :], ACT.Silu)
                    mark("act", act.activation(z[:, RG:RG + 2, :], z[:, RG:RG + 2, :], ACT.Silu), "gates")
                    for i in range(2):
                        tok(l, 10 + i, ps_g[:, 2 + i, :])
                    for j in range(2):
                        after(act, l, "pe", f"ret_kt{j}")
                        mark("act", act.activation(rk_tok[:, :, j * P:(j + 1) * P],
                                                   ps_g[:, j, 0:3 * P].rearrange("p (i c) -> p i c", i=3), ACT.Copy), f"ret_kt{j}")
                    after(act, l, "pe", "att_s11")
                    act.activation(z[:, DQ:DQ + 5, :], y[:, 0:5, :], ACT.Square)
                elif kind == "norms":
                    act.drain()
                    after(act, l, "dve", "ret_xc")
                    mark("act", act.activation(z[:, DQ + 5:DQ + 8, :], y[:, 5:8, :], ACT.Square), "squares")
                    act.preload_act_table(ACT.Sqrt)
                    after(act, l, "dve", "var")
                    mark("act", act.activation(var_h[:, :, :], var_h[:, :, :], ACT.Sqrt), "sqrt")

            with act.Fori(0, DEPTH) as l:
                hi(act, l, 0)
                hi(act, l, 1)
                act.wait_ge(params, l + 1)
                ffn(l, U_F1, 0, 0, U_MIX)
                pre(l, 1, 2, 1)
                for v in range(2):
                    hi(act, l, U_MIX + v + 2)
                for kind, *arg in SCHEDULE:
                    if kind == "part":
                        if arg[2] == KD:
                            hi(act, l, U_MIX + arg[0] + 2)
                    else:
                        mixer_step(l, kind, arg[0] if arg else None)
                for q in HEAD_ORDER:
                    after(act, l, "dve", f"head{q}")
                    split_hi(l, 2, q, y, None)
                for v in range(N_OUT):
                    for n in range(2):
                        y_tile(l, 2 * v + n, 1, 2 * (v % 2) + n, n, 3, l * UNITS + (U_OUT + v + 3) if n == 0 else None, n == 1)
                    if v == N_OUT - 1:
                        root(l, 3)
                    hi(act, l, U_OUT + v + 2)
                act.wait_ge(kv_stored, (l + 1) * 64)
                act.wait_ge(st_stored, (l + 1) * 64)
                ffn(l, U_F2, 4, 3, None)

            for i in range(3):
                act.wait_ge(y_rows, 2 * i + 2)
                if i < 2:
                    act.dma_start(outs["y_prompt"][0, i * P:(i + 1) * P, :], x_in[:, i, :]).then_inc(y_stored, 16)
                else:
                    act.dma_start(outs["y_sample"][0], x_in[64:128, i, :]).then_inc(y_stored, 16)
            act.wait_ge(y_stored, 48)

        @block.vector
        def _(dve):
            dve.sem_inc(w_lo, 2)
            dve.sem_inc(evac, 2)
            dve.sem_inc(y_acc, 2)
            for k in range(KD):
                if k == 2:
                    dve.wait_ge(par_loaded, N_PAR)
                    lam_v = lam_in[:, :, :, :].rearrange("p l (a b) d -> p (l a) b d", b=2)
                    dve.tensor_tensor(lam_p[:, :, :], lam_v[:, :, 0, :], lam_v[:, :, 1, :], ALU.mult)
                    dve.wait_ge(par_mm, 1)
                    dve.tensor_copy(par[:, :, 0:ROWS], ps_m[:, 2, 0:DEPTH * ROWS].rearrange("p (l c) -> p l c", l=DEPTH))
                    dve.drain()
                    dve.tensor_reduce(lam_e[:, :], lam_p[:, :, :], axis=AX.X, op=ALU.add).then_inc(lam_s, 1)
                dve.wait_ge(x_mm, k + 1)
                dve.tensor_copy(x[:, k, :], ps_m[:, k % 2, 0:T]).then_inc(x_new, 1)
            c_lam = 6 * KD + C_LAM
            for l in range(DEPTH):
                dve.tensor_scalar(par[:, l, 6 * KD + C_ATT1:6 * KD + C_ATT1 + 1], par[:, l, 6 * KD + C_ATT:6 * KD + C_ATT + 1],
                                  C("lam")[:, DEPTH + l:DEPTH + l + 1], None, ALU.mult)
            dve.wait_ge(lam_s, 2)
            for l in range(DEPTH):
                dve.tensor_tensor(par[:, l, c_lam:c_lam + 1], lam_e[:, 2 * l:2 * l + 1], lam_e[:, 2 * l + 1:2 * l + 2], ALU.subtract)
            dve.drain()
            for l in range(DEPTH):
                dve.tensor_tensor(par[:, l, c_lam:c_lam + 1], par[:, l, c_lam:c_lam + 1], C("lam")[:, l:l + 1], ALU.add)
            dve.wait_ge(masks_cast, 1)
            then_pass(dve)
            dve.drain()

            def tile(t, k):
                return t[:, k, :] if isinstance(k, int) else t[:, bass.ds(k, 1), :].rearrange("p a t -> p (a t)")

            def split_lo(l, n, k, src, gain, at):
                dve.wait_ge(xn_hi, l * 32 + (8 * n + at + 1))
                if gain is None:
                    i = dve.tensor_tensor(xn_l[:, k, :], src[:, k, :], xn_h[:, k, :], ALU.subtract)
                else:
                    i = dve.scalar_tensor_tensor(xn_l[:, k, :], src[:, k, :], gain_l[:, gain, k:k + 1], xn_h[:, k, :],
                                                 ALU.mult, ALU.subtract)
                i.then_inc(xn_lo, 1)

            def root(l, n, half=False):
                c = 4.0 if half else 1.0
                dve.wait_ge(ss_mm, l * 6 + n + 1)
                dve.tensor_scalar(var[:, 0:3], ps_m[:, 0, 0:3], c / D, c * EPS, ALU.mult, ALU.add).then_inc(ss_var, 1)
                dve.wait_ge(ss_sqrt, l * 6 + n + 1)
                dve.reciprocal(inv[:, 0:3], var[:, 0:3]).then_inc(inv_out, 1)
                dve.wait_ge(rs_mm, l * 6 + n + 1)

            def post(l, n, norm, update):
                for k in range(KD + 2):
                    if update and k < KD:
                        dve.tensor_tensor(y[:, k, :], y[:, k, :], ps_m[:, 1, 0:T], ALU.mult).then_inc(y_norm, 1)
                    if k >= 2 and norm is not None:
                        split_lo(l, n, k - 2, x, norm, k - 2)

            def spread_in(l, norm):
                root(l, norm)
                dve.tensor_copy(rs[:, :], ps_m[:, 1, 0:T])
                dve.drain()

            def add_square(l, m, phase, b):
                dve.drain()
                dve.wait_ge(y_sq, l * 3 * KD + (m + (phase * KD + 1)))
                dve.tensor_tensor(ssum[:, :], ssum[:, :], sq[b][:, :], ALU.add).then_inc(y_acc, 1)

            def ffn(l, u0, g0, norm, following):
                f, phase = norm // 4, norm // 2

                def up_step(v, s, cols):
                    dve.wait_ge(w_used, l * UNITS + (v + (u0 + 3)))
                    dve.tensor_tensor(gate[s][:, :], ps_g[:, 2 * s, 0:T], rs[:, :], ALU.mult).then_inc(up_mul, 1)
                    dve.tensor_tensor(up[s][:, :], ps_g[:, 2 * s + 1, 0:T], rs[:, :], ALU.mult).then_inc(evac, 1)
                    lo_of_unit(dve, l, v + (u0 + 2), s, cols)
                    dve.drain()
                    dve.wait_ge(silu, l * 2 * KF + (v + (KF * f + 1)))
                    dve.tensor_tensor(up[s][:, :], up[s][:, :], gate[s][:, :], ALU.mult).then_inc(prod, 1)
                    dve.wait_ge(hid_hi, l * 2 * KF + (v + (KF * f + 1)))
                    dve.tensor_tensor(tile(hid_l, v), up[s][:, :], tile(hid_h, v), ALU.subtract).then_inc(hid_lo, 1)

                with dve.Fori(0, N_UP // 2 - 1) as j:
                    for s in range(2):
                        up_step(2 * j + s, s, 2 * KD * P)
                for s in range(2):
                    up_step(N_UP - 2 + s, s, HALF_DOWN * P)
                dve.memset(ssum[:, :], 0.0)
                d0 = u0 + N_UP

                def down_tile(m, b):
                    lo_of_unit(dve, l, 2 * m + (d0 + 2), 0, HALF_DOWN * P)
                    add_square(l, m, phase, b)
                    lo_of_unit(dve, l, 2 * m + (d0 + 3), 1, HALF_DOWN * P)

                with dve.Fori(0, KD // 2 - 1) as j:
                    for b in range(2):
                        down_tile(2 * j + b, b)
                down_tile(KD - 2, 0)
                if following is not None:
                    lo(dve, l, following)
                root(l, norm + 1, half=True)
                dve.wait_ge(evac, l * GROUPS + (g0 + N_UP + KD + 2))
                if following is not None:
                    lo(dve, l, following + 1)

            def mixer_step(l, kind, n):
                if kind == "logit":
                    after(dve, l, "act", "abs")
                    mark("dve", dve.tensor_scalar(q_w[:, :], ps_m[:, 0, 0:T], small_l[:, C_BIAS:C_BIAS + 1], 0.0, ALU.add, ALU.min),
                         "minus")
                    dve.tensor_scalar(z[:, GQ, :], z[:, GQ, :], DK_A ** -0.5, None, ALU.mult)
                    dve.drain()
                    after(dve, l, "act", "softplus")
                    dve.tensor_tensor(k_w[:, :], q_w[:, :], wgt[:, :], ALU.subtract)
                    dve.drain()
                    one = C("ones").broadcast_to([P, T_P])
                    dve.tensor_tensor_scan(decay[:, 0:T_P], one[:, 0:T_P], k_w[:, 0:T_P], 0.0, ALU.mult, ALU.add)
                    mark("dve", dve.tensor_tensor_scan(decay[:, T_P:T], one[:, 0:T_S], k_w[:, T_P:T], 0.0, ALU.mult, ALU.add),
                         "decay")
                elif kind == "level":
                    flat = scores[:, :, :, :].rearrange("p h b c -> p h (b c)")
                    if n == 0:
                        dve.wait_ge(mem_set, l + 1)
                        then_pass(dve)
                        after(dve, l, "pe", "level0")
                        i = dve.tensor_copy(scores[:, :, 3, :], ps_m[:, :, 3 * P:4 * P])
                    else:
                        dve.drain()
                        after(dve, l, "pe", f"level{n}")
                        then_pass(dve)
                        for a, b in (((0, P), (2 * P, 3 * P)) if n == 1 else ((0, 3 * P),)):
                            m = mask[:, n - 1:n, a:b].broadcast_to([P, H, b - a])
                            i = dve.copy_predicated(flat[:, :, a:b], m, ps_m[:, :, a:b])
                    mark("dve", i, f"score{n}")
                elif kind == "gla_keys":
                    after(dve, l, "act", "from_start")
                    mark("dve", dve.tensor_tensor(q_s[:, 0, :], q_s[:, 0, :], z[:, GQ, T_P:T], ALU.mult), "q_start")
                    after(dve, l, "act", "to_end")
                    mark("dve", dve.tensor_tensor(k_w[:, :], z[:, GK, :], wgt[:, :], ALU.mult), "k_end")
                elif kind == "gla_out":
                    after(dve, l, "pe", "gla_state")
                    dve.wait_ge(past_in, (l + 1) * 64)
                    for h in range(H):
                        r, c = slice(32 * h, 32 * h + 32), slice(64 * h, 64 * h + 64)
                        dve.tensor_copy(st_a[r, 0, :], ps_m[r, 0, c])
                        i = dve.scalar_tensor_tensor(st_a[r, 1, :], s0_a[r, :], tiny[r, 3:4], ps_m[r, 1, c], ALU.mult, ALU.add)
                    mark("dve", i, "gla_state")
                    after(dve, l, "pe", "gla_o")
                    mark("dve", dve.tensor_copy(y[:, 0:2, :], ps_m[:, 2:4, 0:T]), "gla_o")
                elif kind == "att":
                    if n < 12:
                        h, b = ATT[n]
                        keys, s = KEYS[b] * P, n % 2
                        pr = probs[:, s, :, 0:keys]
                        bias = C(f"bias{h}")[:, BIAS_AT[b]:BIAS_AT[b] + keys].rearrange("p (o c) -> p o c", o=1) \
                            .broadcast_to([P, 2, keys])
                        after(dve, l, "pe", f"att_s{n}")
                        dve.scalar_tensor_tensor(pr, ps_m[:, 0:2, 0:keys], DK_D ** -0.5, bias, ALU.mult, ALU.add)
                        dve.drain()
                        mark("dve", dve.tensor_reduce(tiny[:, 8 + 2 * s:10 + 2 * s], pr, axis=AX.X, op=ALU.max, negate=True),
                             f"att_max{n}")
                    if 1 <= n <= 12:
                        keys, s = KEYS[ATT[n - 1][1]] * P, (n - 1) % 2
                        inv_p = tiny[:, 16 + 2 * s:18 + 2 * s]
                        after(dve, l, "act", f"att_e{n - 1}")
                        dve.reciprocal(inv_p, tiny[:, 12 + 2 * s:14 + 2 * s])
                        dve.drain()
                        dve.tensor_scalar(probs[:, s, 1, 0:keys], probs[:, s, 1, 0:keys], inv_p[:, 1:2], small_l[:, C_LAM:C_LAM + 1],
                                          ALU.mult, ALU.mult)
                        dve.drain()
                        mark("dve", dve.scalar_tensor_tensor(probs[:, s, 0, 0:keys], probs[:, s, 0, 0:keys], inv_p[:, 0:1],
                                                             probs[:, s, 1, 0:keys], ALU.mult, ALU.subtract), f"att_a{n - 1}")
                elif kind == "rot":
                    c = 1.0 if n < 2 else DK_R ** -0.5
                    zt = z[:, RQ + n, :]
                    after(dve, l, "pe", f"rot{n}")
                    dve.scalar_tensor_tensor(wgt[:, :], ps_m[:, 2, 0:T], c, C("sin"), ALU.mult, ALU.mult)
                    dve.scalar_tensor_tensor(zt, zt, c, C("cos"), ALU.mult, ALU.mult)
                    dve.drain()
                    mark("dve", dve.tensor_tensor(zt, zt, wgt[:, :], ALU.add), f"rot{n}")
                elif kind == "ret_s":
                    after(dve, l, "pe", f"ret_s{n}")
                    mark("dve", dve.tensor_tensor(scores[:, n, :, :].rearrange("p b c -> p (b c)"), ps_m[:, 2, :], C(f"dec{n}"),
                                                  ALU.mult), f"ret_s{n}")
                elif kind == "ret_keys":
                    dve.drain()
                    for j in range(2):
                        i = dve.tensor_tensor(q_s[:, j, :], z[:, RQ + j, T_P:T], C(f"q_dec{j}"), ALU.mult)
                    mark("dve", i, "ret_q")
                    for j, t in enumerate((k_w, wgt)):
                        i = dve.tensor_tensor(t[:, :], z[:, RK + j, :], C(f"k_dec{j}"), ALU.mult)
                    mark("dve", i, "ret_k")
                elif kind == "ret_out":
                    after(dve, l, "pe", "ret_state")
                    for j in range(2):
                        for hh in range(2):
                            r = slice(64 * hh, 64 * hh + 64)
                            g = float((1.0 - 2.0 ** (-5.0 - (2 * j + hh))) ** T_S)
                            dve.tensor_copy(st_r[r, 0, j, :], ps_g[r, j, 64 * hh:64 * hh + 64])
                            i = dve.scalar_tensor_tensor(st_r[r, 1, j, :], s0_r[r, j, :], g, ps_g[r, j, P + 64 * hh:P + 64 * hh + 64],
                                                         ALU.mult, ALU.add)
                    mark("dve", i, "ret_state")
                    after(dve, l, "pe", "ret_o")
                    mark("dve", dve.tensor_copy(y[:, 6:8, :], ps_m[:, 0:2, 0:T]), "ret_o")
                    dve.drain()
                    after(dve, l, "pe", "ret_mu")
                    mark("dve", dve.tensor_tensor(y[:, 6:8, :], y[:, 6:8, :], ps_g[:, 2:4, 0:T], ALU.subtract), "ret_xc")
                elif kind == "norms":
                    after(dve, l, "pe", "ms")
                    mark("dve", dve.tensor_scalar(var_h[:, :, :], ps_g[:, 0, 0:36].rearrange("p (i h) -> p i h", i=3), EPS, None,
                                                  ALU.add), "var")
                    after(dve, l, "act", "sqrt")
                    mark("dve", dve.reciprocal(inv_h[:, :, :], var_h[:, :, :]), "inv")
                    gains_at = (C_GLA, C_GLA + 1, C_ATT1, C_ATT1, C_ATT1, C_ATT1, C_RET, C_RET + 1)
                    for j, q in enumerate(HEAD_ORDER):
                        after(dve, l, "pe", f"spread{q}")
                        i = dve.scalar_tensor_tensor(y[:, q, :], y[:, q, :], small_l[:, gains_at[q]:gains_at[q] + 1],
                                                     ps_m[:, 1 + j % 2, 0:T], ALU.mult, ALU.mult)
                        if q in (0, 1, 6, 7):
                            dve.drain()
                            g = z[:, GR + q, :] if q < 2 else z[:, RG + q - 6, :]
                            i = dve.tensor_tensor(y[:, q, :], y[:, q, :], g, ALU.mult)
                        mark("dve", i, f"head{q}")
                        if j:
                            split_lo(l, 2, HEAD_ORDER[j - 1], y, None, j - 1)
                    split_lo(l, 2, HEAD_ORDER[-1], y, None, KD - 1)

            with dve.Fori(0, DEPTH) as l:
                dve.tensor_copy(par_l[:, :], par[:, bass.ds(l, 1), :].rearrange("p o a -> p (o a)"))
                dve.tensor_copy(a2_l[:, :], a2[:, bass.ds(l, 1), :].rearrange("p o a -> p (o a)")).then_inc(params, 1)
                dve.drain()
                lo(dve, l, 0)
                lo(dve, l, 1)
                post(l, 0, 0, False)
                spread_in(l, 0)
                ffn(l, U_F1, G_F1, 0, U_MIX)
                post(l, 1, 2, True)
                spread_in(l, 2)
                dve.wait_ge(tables_loaded, 16)
                dve.tensor_tensor(alr[0:RANK, :], ps_g[0:RANK, 0, 0:T], rs[0:RANK, :], ALU.mult).then_inc(evac, 1)
                rs2 = rs[:, :].rearrange("p (o t) -> p o t", o=1).broadcast_to([P, 2, T])

                def z_tiles(v):
                    s, t = v % 2, UNIT_TILE[v]
                    dve.wait_ge(w_used, l * UNITS + (U_MIX + v + 3))
                    dve.tensor_tensor(z[:, t:t + 2, :], ps_g[:, 2 * s:2 * s + 2, 0:T], rs2, ALU.mult).then_inc(evac, 1)

                z_tiles(1)
                lo(dve, l, U_MIX + 2)
                for kind, *arg in SCHEDULE:
                    if kind == "part":
                        v, k0, k1 = arg
                        if k0 == 0:
                            lo(dve, l, U_MIX + v + 1)
                        if k1 == KD:
                            z_tiles(v)
                    else:
                        mixer_step(l, kind, arg[0] if arg else None)
                lo(dve, l, U_OUT + 1)
                dve.memset(ssum[:, :], 0.0)
                for v in range(N_OUT):
                    for n in range(2):
                        if 2 * v + n < KD - 1:
                            add_square(l, 2 * v + n, 1, n)
                    if v == N_OUT - 1:
                        root(l, 3)
                    lo(dve, l, U_OUT + v + 2)
                dve.wait_ge(evac, l * GROUPS + (G_OUT + N_OUT + 2))
                post(l, 3, 4, True)
                spread_in(l, 4)
                ffn(l, U_F2, G_F2, 4, None)
                post(l, 0, None, True)

            dve.wait_ge(x_new, (3 * DEPTH + 1) * KD)
            for n in range(6):
                i, half = n // 2, n % 2
                dve.wait_ge(y_mm, n + 1)
                dve.tensor_copy(x_in[:, i, half * 512:(half + 1) * 512], ps_m[:, half, :]).then_inc(y_rows, 1)

        for k, n in reached.items():
            assert n == len(MILESTONES[k]), (k, n, len(MILESTONES[k]))


_INS = ["x_prompt", "x_sample", "cache_diff_k", "cache_diff_v", "state_gla", "state_ret",
        "ffn1_norm_pre", "ffn1_w_up", "ffn1_w_down", "ffn1_norm_post", "mix_norm_pre", "w_in", "w_gla_a2", "b_gla_a",
        "gla_norm", "diff_lambda", "diff_subln", "ret_norm", "w_out", "mix_norm_post",
        "ffn2_norm_pre", "ffn2_w_up", "ffn2_w_down", "ffn2_norm_post"]
_OUTS = {
    "y_prompt": (1, T_P, D), "y_sample": (1, T_S, D),
    "new_k_prompt": (DEPTH, 1, T_P, H, 2 * DK_D), "new_v_prompt": (DEPTH, 1, T_P, H, DV_D),
    "state_gla_prompt": (DEPTH, 1, H, DK_A, DV_A), "state_ret_prompt": (DEPTH, 1, H, DK_R, DV_R),
    "new_k_sample": (DEPTH, 1, T_S, H, 2 * DK_D), "new_v_sample": (DEPTH, 1, T_S, H, DV_D),
    "state_gla_sample": (DEPTH, 1, H, DK_A, DV_A), "state_ret_sample": (DEPTH, 1, H, DK_R, DV_R),
}


def kernel(**inputs):
    import numpy as _np
    import concourse.bacc as _bacc
    from concourse import mybir as _mybir
    from concourse.bass_utils import run_bass_kernel_spmd as _run

    nc = _bacc.Bacc("TRN2", target_bir_lowering=False, num_devices=1)
    tables, table_at, masks = constants()
    arrays, ins, outs = {}, {}, {}
    for name in _INS + ["tables", "masks"]:
        a = _np.ascontiguousarray(tables if name == "tables" else masks if name == "masks" else inputs[name])
        arrays[f"in_{name}_dram"] = a
        ins[name] = nc.dram_tensor(f"in_{name}_dram", a.shape, _mybir.dt.from_np(a.dtype), kind="ExternalInput").ap()
    for name, shape in _OUTS.items():
        outs[name] = nc.dram_tensor(f"out_{name}_dram", shape, F32, kind="ExternalOutput").ap()
    build(nc, ins, outs, table_at)
    r = _run(nc, [arrays], core_ids=[0])
    return tuple(r.results[0][f"out_{name}_dram"] for name in _OUTS)
```
